# Optimizing a Trainium2 kernel written in Bass

```python
import functools
import jax, jax.numpy as jnp
from jax import lax
import numpy as np

D_MODEL = 2048
BATCH = 1
SEQ = 256
DEPTH = 2
DEC_BATCH = 1
DEC_SEQ = 64
PAST_LEN = 256

CHUNK = 64
N_A = (DEPTH + 1) // 2
N_C = DEPTH // 2
EPS = 1e-6
RET_HEADS = 8
RET_DK = 128
RET_DV = 128
RET_WIDTH = RET_HEADS * RET_DV
POOL_WINDOWS = (2, 4, 8, 16)
POOL_GROUPS = 4
POOL_WIDTH = D_MODEL // 2
POOL_GROUP_DIM = POOL_WIDTH // POOL_GROUPS
POOL_BUF = max(POOL_WINDOWS) - 1
IN_A = 2 * RET_HEADS * RET_DK + 2 * RET_WIDTH + POOL_WIDTH
ML_HEADS = 8
ML_DK = 128
ML_DV = 256
ML_QK = ML_HEADS * ML_DK
ML_V = ML_HEADS * ML_DV
ML_CONV = 4
IN_C = 2 * ML_QK + 2 * ML_V + 2 * ML_HEADS
D_FF = 5632
FFN_CONV = 3

kernel_name = 'streaming_retention_pool_mlstm_convffn'

def rms_norm(x, g):
    xf = x.astype(jnp.float32)
    y = xf * lax.rsqrt(jnp.mean(xf * xf, -1, keepdims=True) + EPS)
    return (y * g.astype(jnp.float32)).astype(x.dtype)

def head_rms(x):
    return x * lax.rsqrt(jnp.mean(x * x, -1, keepdims=True) + EPS)

def rotary(x, pos):
    half = x.shape[-1] // 2
    inv = 1.0 / (10000.0 ** jnp.linspace(0.0, 1.0, half, dtype=jnp.float32))
    ang = pos.astype(jnp.float32)[:, None] * inv[None, :]
    cos = jnp.cos(ang)[None, :, None, :]
    sin = jnp.sin(ang)[None, :, None, :]
    xf = x.astype(jnp.float32)
    x1, x2 = xf[..., :half], xf[..., half:]
    return jnp.concatenate([x1 * cos - x2 * sin, x1 * sin + x2 * cos], -1)

def causal_dwconv(ext, w, L):
    acc = ext[:, 0:L] * w[0]
    for j in range(1, w.shape[0]):
        acc = acc + ext[:, j:j + L] * w[j]
    return acc

def run_chunks(step, carry, seqs):
    L = seqs[0].shape[1]
    if L <= CHUNK:
        return step(carry, *seqs)
    n = L // CHUNK
    split = lambda a: jnp.moveaxis(a.reshape(a.shape[0], n, CHUNK, *a.shape[2:]), 1, 0)
    carry, ys = lax.scan(lambda c, xs: step(c, *xs), carry, tuple(split(a) for a in seqs))
    ys = jnp.moveaxis(ys, 0, 1)
    return carry, ys.reshape(ys.shape[0], L, *ys.shape[3:])

def retention_chunk(S, q, k, v, log_gamma):
    L = q.shape[1]
    idx = jnp.arange(L, dtype=jnp.float32)
    diff = idx[:, None] - idx[None, :]
    dec = jnp.where(diff >= 0, jnp.exp(log_gamma[:, None, None] * jnp.maximum(diff, 0.0)), 0.0)
    s = jnp.einsum('blhd,bmhd->bhlm', q, k) * dec
    intra = jnp.einsum('bhlm,bmhe->blhe', s, v)
    q_dec = jnp.exp((idx[:, None] + 1.0) * log_gamma)
    inter = jnp.einsum('blhd,bhde->blhe', q, S) * q_dec[None, :, :, None]
    k_dec = jnp.exp((L - 1.0 - idx[:, None]) * log_gamma)
    S_new = (jnp.exp(L * log_gamma)[None, :, None, None] * S
             + jnp.einsum('blhd,blhe->bhde', k * k_dec[None, :, :, None], v))
    return S_new, intra + inter

def mlstm_chunk(carry, q, k, v, ig, lf):
    C, n, m = carry
    L = q.shape[1]
    causal = jnp.tril(jnp.ones((L, L), bool))
    b = jnp.moveaxis(jnp.cumsum(lf, 1), 1, 2)
    i = jnp.moveaxis(ig, 1, 2)
    dlog = jnp.where(causal, b[..., :, None] - b[..., None, :] + i[..., None, :], -jnp.inf)
    inter_log = b + m[..., None]
    m_t = jnp.maximum(inter_log, jnp.max(dlog, -1))
    dw = jnp.exp(dlog - m_t[..., None])
    iw = jnp.exp(inter_log - m_t)
    s = jnp.einsum('blhd,bmhd->bhlm', q, k) * dw
    iw_t = jnp.moveaxis(iw, 1, 2)[..., None]
    num = jnp.einsum('bhlm,bmhe->blhe', s, v) + jnp.einsum('blhd,bhde->blhe', q, C) * iw_t
    den = jnp.sum(s, -1) + jnp.einsum('blhd,bhd->bhl', q, n) * iw
    floor = jnp.maximum(jnp.abs(den), jnp.exp(-m_t))
    h = num / jnp.moveaxis(floor, 1, 2)[..., None]
    m_L = m_t[..., -1]
    w_end = jnp.exp(b[..., -1:] - b + i - m_L[..., None])
    decay = jnp.exp(b[..., -1] + m - m_L)
    C_new = decay[..., None, None] * C + jnp.einsum('bhs,bshd,bshe->bhde', w_end, k, v)
    n_new = decay[..., None] * n + jnp.einsum('bhs,bshd->bhd', w_end, k)
    return (C_new, n_new, m_L), h

def multiscale_pool(u, buf, pos):
    Bn, L, P = u.shape
    ext = jnp.concatenate([buf.astype(u.dtype), u], 1)
    cz = jnp.concatenate([jnp.zeros((Bn, 1, P), jnp.float32), jnp.cumsum(ext.astype(jnp.float32), 1)], 1)
    cz = cz.reshape(Bn, POOL_BUF + L + 1, POOL_GROUPS, POOL_GROUP_DIM)
    end = cz[:, POOL_BUF + 1:]
    means = []
    for j, w in enumerate(POOL_WINDOWS):
        start = cz[:, POOL_BUF + 1 - w:POOL_BUF + 1 - w + L, j]
        cnt = jnp.minimum(pos + 1, w).astype(jnp.float32)[None, :, None]
        means.append((end[:, :, j] - start) / cnt)
    mean = jnp.stack(means, 2)
    pooled = mean - u.reshape(Bn, L, POOL_GROUPS, POOL_GROUP_DIM).astype(jnp.float32)
    return pooled, ext[:, -POOL_BUF:]

def retention_pool_mixer(h, pos, S0, pool_buf, w_in, w_pool, pool_scale, w_out):
    Bn, L, _ = h.shape
    proj = h @ w_in
    qw = RET_HEADS * RET_DK
    q = proj[..., :qw].reshape(Bn, L, RET_HEADS, RET_DK)
    k = proj[..., qw:2 * qw].reshape(Bn, L, RET_HEADS, RET_DK)
    v = proj[..., 2 * qw:2 * qw + RET_WIDTH].reshape(Bn, L, RET_HEADS, RET_DV).astype(jnp.float32)
    g = proj[..., 2 * qw + RET_WIDTH:2 * qw + 2 * RET_WIDTH].astype(jnp.float32)
    u = proj[..., 2 * qw + 2 * RET_WIDTH:]
    q = rotary(q, pos)
    k = rotary(k, pos) * (RET_DK ** -0.5)
    log_gamma = jnp.log1p(-(2.0 ** (-5.0 - jnp.arange(RET_HEADS, dtype=jnp.float32))))
    step = functools.partial(retention_chunk, log_gamma=log_gamma)
    S, o = run_chunks(step, S0.astype(jnp.float32), (q, k, v))
    ret = head_rms(o).reshape(Bn, L, RET_WIDTH) * jax.nn.silu(g)
    pooled, new_buf = multiscale_pool(u, pool_buf, pos)
    pool = jnp.einsum('blgc,gcd->blgd', pooled, w_pool).reshape(Bn, L, POOL_WIDTH) * pool_scale
    y = jnp.concatenate([ret.astype(h.dtype), pool.astype(h.dtype)], -1) @ w_out
    return y, S, new_buf

def mlstm_mixer(h, conv_buf, C0, n0, m0, w_in, conv_w, conv_b, b_i, b_f, norm_g, w_out):
    Bn, L, _ = h.shape
    proj = h @ w_in
    qk_pre = proj[..., :2 * ML_QK]
    v = proj[..., 2 * ML_QK:2 * ML_QK + ML_V].reshape(Bn, L, ML_HEADS, ML_DV).astype(jnp.float32)
    o = proj[..., 2 * ML_QK + ML_V:2 * ML_QK + 2 * ML_V].astype(jnp.float32)
    ig = proj[..., 2 * ML_QK + 2 * ML_V:2 * ML_QK + 2 * ML_V + ML_HEADS].astype(jnp.float32) + b_i
    fg = proj[..., 2 * ML_QK + 2 * ML_V + ML_HEADS:].astype(jnp.float32) + b_f
    ext = jnp.concatenate([conv_buf.astype(qk_pre.dtype), qk_pre], 1)
    qk = jax.nn.silu((causal_dwconv(ext, conv_w, L) + conv_b).astype(jnp.float32))
    q = qk[..., :ML_QK].reshape(Bn, L, ML_HEADS, ML_DK)
    k = qk[..., ML_QK:].reshape(Bn, L, ML_HEADS, ML_DK) * (ML_DK ** -0.5)
    lf = jax.nn.log_sigmoid(fg)
    carry0 = (C0.astype(jnp.float32), n0.astype(jnp.float32), m0.astype(jnp.float32))
    (C, n, m), hh = run_chunks(mlstm_chunk, carry0, (q, k, v, ig, lf))
    hh = head_rms(hh) * norm_g.astype(jnp.float32).reshape(ML_HEADS, ML_DV)
    y = (hh.reshape(Bn, L, ML_V) * jax.nn.sigmoid(o)).astype(h.dtype) @ w_out
    return y, C, n, m, ext[:, -(ML_CONV - 1):]

def conv_ffn(h, buf, w_up, w_gate, conv_w, conv_b, w_down):
    L = h.shape[1]
    up = h @ w_up
    gate = h @ w_gate
    ext = jnp.concatenate([buf.astype(gate.dtype), gate], 1)
    act = jax.nn.gelu(causal_dwconv(ext, conv_w, L) + conv_b)
    return (act * up) @ w_down, ext[:, -(FFN_CONV - 1):]

def trunk(x, pos, ret_S, pool_buf, ml_C, ml_n, ml_m, ml_conv, ffn_buf, p):
    o_S, o_pool, o_C, o_n, o_m, o_conv, o_ffn = [], [], [], [], [], [], []
    for l in range(DEPTH):
        h = rms_norm(x, p['norm_mix'][l])
        if l % 2 == 0:
            a = l // 2
            y, S, pb = retention_pool_mixer(h, pos, ret_S[a], pool_buf[a], p['w_in_a'][a], p['w_pool'][a],
                                            p['pool_scale'][a], p['w_out_a'][a])
            o_S.append(S)
            o_pool.append(pb)
        else:
            c = l // 2
            y, C, n, m, cb = mlstm_mixer(h, ml_conv[c], ml_C[c], ml_n[c], ml_m[c], p['w_in_c'][c],
                                         p['conv_c_w'][c], p['conv_c_b'][c], p['b_i'][c], p['b_f'][c],
                                         p['ml_norm'][c], p['w_out_c'][c])
            o_C.append(C)
            o_n.append(n)
            o_m.append(m)
            o_conv.append(cb)
        x = x + y
        y, fb = conv_ffn(rms_norm(x, p['norm_ffn'][l]), ffn_buf[l], p['w_up'][l], p['w_gate'][l],
                         p['ffn_conv_w'][l], p['ffn_conv_b'][l], p['w_down'][l])
        o_ffn.append(fb)
        x = x + y
    return (rms_norm(x, p['norm_final']), jnp.stack(o_S), jnp.stack(o_pool), jnp.stack(o_C),
            jnp.stack(o_n), jnp.stack(o_m), jnp.stack(o_conv), jnp.stack(o_ffn))

def setup_inputs(seed: int = 0) -> dict:
    key = jax.random.key(seed)
    ks = iter(jax.random.split(key, 40))
    nrm = lambda shape, scale: scale * jax.random.normal(next(ks), shape, jnp.float32)
    return {
        'x_prompt': nrm((BATCH, SEQ, D_MODEL), 1.0),
        'x_sample': nrm((DEC_BATCH, DEC_SEQ, D_MODEL), 1.0),
        'state_ret': nrm((N_A, DEC_BATCH, RET_HEADS, RET_DK, RET_DV), 0.3),
        'cache_pool': nrm((N_A, DEC_BATCH, POOL_BUF, POOL_WIDTH), 1.0),
        'state_mlstm_C': nrm((N_C, DEC_BATCH, ML_HEADS, ML_DK, ML_DV), 0.3),
        'state_mlstm_n': nrm((N_C, DEC_BATCH, ML_HEADS, ML_DK), 0.3),
        'state_mlstm_m': nrm((N_C, DEC_BATCH, ML_HEADS), 1.0),
        'cache_mlstm_conv': nrm((N_C, DEC_BATCH, ML_CONV - 1, 2 * ML_QK), 1.0),
        'cache_ffn_conv': nrm((DEPTH, DEC_BATCH, FFN_CONV - 1, D_FF), 1.0),
        'norm_mix': 1.0 + nrm((DEPTH, D_MODEL), 0.02),
        'norm_ffn': 1.0 + nrm((DEPTH, D_MODEL), 0.02),
        'norm_final': 1.0 + nrm((D_MODEL,), 0.02),
        'w_in_a': nrm((N_A, D_MODEL, IN_A), D_MODEL ** -0.5),
        'w_pool': nrm((N_A, POOL_GROUPS, POOL_GROUP_DIM, POOL_GROUP_DIM), POOL_GROUP_DIM ** -0.5),
        'pool_scale': 1.0 + nrm((N_A, POOL_WIDTH), 0.1),
        'w_out_a': nrm((N_A, RET_WIDTH + POOL_WIDTH, D_MODEL), (RET_WIDTH + POOL_WIDTH) ** -0.5),
        'w_in_c': nrm((N_C, D_MODEL, IN_C), D_MODEL ** -0.5),
        'conv_c_w': nrm((N_C, ML_CONV, 2 * ML_QK), 0.5),
        'conv_c_b': nrm((N_C, 2 * ML_QK), 0.01),
        'b_i': nrm((N_C, ML_HEADS), 0.1),
        'b_f': jnp.linspace(3.0, 6.0, ML_HEADS, dtype=jnp.float32)[None, :] + nrm((N_C, ML_HEADS), 0.1),
        'ml_norm': 1.0 + nrm((N_C, ML_V), 0.02),
        'w_out_c': nrm((N_C, ML_V, D_MODEL), ML_V ** -0.5),
        'w_up': nrm((DEPTH, D_MODEL, D_FF), D_MODEL ** -0.5),
        'w_gate': nrm((DEPTH, D_MODEL, D_FF), D_MODEL ** -0.5),
        'ffn_conv_w': nrm((DEPTH, FFN_CONV, D_FF), 0.6),
        'ffn_conv_b': nrm((DEPTH, D_FF), 0.01),
        'w_down': nrm((DEPTH, D_FF, D_MODEL), D_FF ** -0.5),
    }

def reference(x_prompt, x_sample, state_ret, cache_pool, state_mlstm_C, state_mlstm_n, state_mlstm_m,
              cache_mlstm_conv, cache_ffn_conv, norm_mix, norm_ffn, norm_final, w_in_a, w_pool, pool_scale,
              w_out_a, w_in_c, conv_c_w, conv_c_b, b_i, b_f, ml_norm, w_out_c, w_up, w_gate, ffn_conv_w,
              ffn_conv_b, w_down):
    p = dict(norm_mix=norm_mix, norm_ffn=norm_ffn, norm_final=norm_final, w_in_a=w_in_a, w_pool=w_pool,
             pool_scale=pool_scale, w_out_a=w_out_a, w_in_c=w_in_c, conv_c_w=conv_c_w, conv_c_b=conv_c_b,
             b_i=b_i, b_f=b_f, ml_norm=ml_norm, w_out_c=w_out_c, w_up=w_up, w_gate=w_gate,
             ffn_conv_w=ffn_conv_w, ffn_conv_b=ffn_conv_b, w_down=w_down)
    f32 = jnp.float32
    B0, T0 = x_prompt.shape[0], x_prompt.shape[1]
    dt = x_prompt.dtype
    pos_p = jnp.arange(T0, dtype=jnp.int32)
    (y_prompt, p_ret, p_pool, p_C, p_n, p_m, p_conv, p_ffn) = trunk(
        x_prompt, pos_p,
        jnp.zeros((N_A, B0, RET_HEADS, RET_DK, RET_DV), f32),
        jnp.zeros((N_A, B0, POOL_BUF, POOL_WIDTH), dt),
        jnp.zeros((N_C, B0, ML_HEADS, ML_DK, ML_DV), f32),
        jnp.zeros((N_C, B0, ML_HEADS, ML_DK), f32),
        jnp.zeros((N_C, B0, ML_HEADS), f32),
        jnp.zeros((N_C, B0, ML_CONV - 1, 2 * ML_QK), dt),
        jnp.zeros((DEPTH, B0, FFN_CONV - 1, D_FF), dt), p)
    pos_s = PAST_LEN + jnp.arange(x_sample.shape[1], dtype=jnp.int32)
    (y_sample, s_ret, s_pool, s_C, s_n, s_m, s_conv, s_ffn) = trunk(
        x_sample, pos_s, state_ret, cache_pool, state_mlstm_C, state_mlstm_n, state_mlstm_m,
        cache_mlstm_conv, cache_ffn_conv, p)
    return (y_prompt, y_sample, p_ret, p_pool, p_C, p_n, p_m, p_conv, p_ffn,
            s_ret, s_pool, s_C, s_n, s_m, s_conv, s_ffn)


_drawn_inputs = setup_inputs


def setup_inputs(seed=0):
    import zlib

    import numpy as np

    out = dict(_drawn_inputs(seed))
    spreads = {}
    factors = {'norm_final': 2.91, 'ml_norm': 7.11, 'ffn_conv_b': 7.157}
    for name, (base, spread) in spreads.items():
        noise = np.random.default_rng([zlib.crc32(name.encode()), seed]).standard_normal(out[name].shape)
        drawn = base * np.exp(spread * noise) if base else spread * noise
        out[name] = __import__('jax').numpy.asarray(drawn.astype(out[name].dtype))
    for name, factor in factors.items():
        out[name] = (out[name] * factor).astype(out[name].dtype)
    return out
```

```python
from contextlib import ExitStack, contextmanager

import numpy as np

import concourse.bass as bass
from concourse import mybir

F32 = mybir.dt.float32
F32R = mybir.dt.float32r
ALU = mybir.AluOpType
ACT = mybir.ActivationFunctionType

P = 128
D_MODEL, SEQ, DEC_SEQ, PAST_LEN = 2048, 256, 64, 256
T = SEQ + DEC_SEQ
HEADS, DK = 8, 128
RET_DV, ML_DV = 128, 256
POOL_WIDTH, POOL_GROUPS, POOL_BUF = 1024, 4, 15
ML_CONV, FFN_CONV = 4, 3
D_FF, EPS = 5632, 1e-6
KT = D_MODEL // P
FT = D_FF // P
BLOCKS = (16, 16, 12)
RING = 4
UK, UM = 4, 2
UW = UK * UM * P
AHEAD = RING - 1

U_HEADS = 0
U_POOL = U_HEADS + HEADS * 8
U_OUTA = U_POOL + POOL_GROUPS * 4
U_FFN0 = U_OUTA + KT // UM * 4
FFN_UNITS = FT // UM * 8 + KT // UM * FT // UK
U_GATES = U_FFN0 + FFN_UNITS
U_ML = U_GATES + 4
U_OUTC = U_ML + HEADS * 12
U_FFN1 = U_OUTC + KT // UM * 4
UNITS = U_FFN1 + FFN_UNITS

PR_HEADS = 0
PR_POOL = PR_HEADS + HEADS * 2
PR_OUTA = PR_POOL + POOL_GROUPS
PR_FFN0 = PR_OUTA + KT // UM
FFN_PAIRS = FT + len(BLOCKS) * KT // UM
PR_GATES = PR_FFN0 + FFN_PAIRS
PR_ML = PR_GATES + 1
PR_OUTC = PR_ML + HEADS * 3
PR_FFN1 = PR_OUTC + KT // UM
PR_END = PR_FFN1 + FFN_PAIRS


class Layout:

    def __init__(self):
        self.at, self.width = {}, 0

    def add(self, name, width):
        self.at[name] = (self.width, width)
        self.width += width

    def __getitem__(self, name):
        return self.at[name][0]


COL = Layout()
for name, width in (("mix0", KT), ("mix1", KT), ("ffn0", KT), ("ffn1", KT), ("final", KT), ("pool_scale", 8),
                    ("conv_c_w", 16 * ML_CONV), ("conv_c_b", 16), ("ml_norm", 16),
                    ("ffn_w0", FT * FFN_CONV), ("ffn_w1", FT * FFN_CONV), ("ffn_b0", FT), ("ffn_b1", FT),
                    ("conv_hist", 16 * 3), ("pool_hist", 8 * POOL_BUF), ("ffn_hist0", FT * 2), ("ffn_hist1", FT * 2),
                    ("b_i", 1), ("b_f", 1), ("m0", 1), ("n0", HEADS)):
    COL.add(name, width)

CON = Layout()
for name, width in (("cos", T), ("sin", T), ("late", SEQ), ("ident", P), ("ones", P), ("kdec", 3 * HEADS),
                    ("gamma_l", HEADS), ("pool_fix", POOL_GROUPS * 16), ("eps", 1), ("eps4", 1)):
    CON.add(name, width)
RET_TABLE = SEQ + DEC_SEQ


class Count:

    def __init__(self, sem):
        self.sem, self.base, self.n, self.i, self.per = sem, 0, 0, None, 0

    def inc(self, ins):
        ins.then_inc(self.sem, 1)
        self.n += 1

    def value(self):
        known = self.base + self.n
        return known if self.i is None else self.i * self.per + known


@contextmanager
def counted(engine, trips, per):
    for c, k in per:
        assert c.i is None
        c.base, c.n = c.base + c.n, 0
    with engine.Fori(0, trips) as i:
        for c, k in per:
            c.i, c.per = i, k
        yield i
    for c, k in per:
        assert c.n == k, (c.sem, c.n, k)
        c.base, c.n, c.i, c.per = c.base + k * trips, 0, None, 0


class Unit:

    def __init__(self, first, i=None, per=0):
        assert per % RING == 0
        self.first, self.i, self.per = first, i, per
        self.slot = first % RING

    def plus(self, k):
        return Unit(self.first + k, self.i, self.per)

    def number(self, add=0):
        return self.first + add if self.i is None else self.i * self.per + (self.first + add)

    def turn(self, scale, add):
        known = self.first // RING * scale + add
        return known if self.i is None else self.i * (self.per // RING * scale) + known

    @property
    def exists(self):
        return self.first < UNITS


def trunk_kernel(nc, x_in, weights, w_pool_in, cols_in, consts_in, ret_tables_in, ret_state_in, ml_state_in,
                 y_out, ret_out, pool_out, c_out, m_out, conv_out, ffn_out):
    with ExitStack() as ctx:
        def sb(name, width, dt=F32, parts=P):
            return ctx.enter_context(nc.sbuf_tensor(name, [parts, width], dt))

        def sem(name):
            return ctx.enter_context(nc.semaphore(name))

        x = sb("x", KT * T)
        a_hi, a_lo = sb("a_hi", KT * T, F32R), sb("a_lo", KT * T, F32R)
        b_hi, b_lo = sb("b_hi", KT * T, F32R), sb("b_lo", KT * T, F32R)
        raw = sb("raw", RING * UW)
        w_hi, w_lo = sb("w_hi", RING * UW, F32R), sb("w_lo", RING * UW, F32R)
        cols = sb("cols", COL.width)
        con = sb("con", CON.width)
        rt = sb("rt", T)
        sq_sum, sq_one = sb("sq_sum", T), sb("sq_one", T)
        std = sb("std", T)
        ffn_rows = sb("ffn_rows", 2 * FT * 4)
        WORK = 11400
        work = sb("work", WORK)
        used = [0]

        def piece(width, restart=False):
            if restart:
                used[0] = 0
            at = used[0]
            used[0] += width
            assert used[0] <= WORK, used
            return work[:, at:at + width]

        EXT = POOL_BUF + SEQ + POOL_BUF + DEC_SEQ
        SC = SEQ + P + DEC_SEQ
        w_pool = piece(2048, restart=True)
        sin_r = piece(T)
        ret_table, ret_s0 = piece(RET_TABLE), piece(RET_DV)
        heads_only = used[0]
        q_t, k_t, q_swap, k_swap, cos_r = (piece(T) for _ in range(5))
        v_t, z_g, tanh_g, gate = (piece(T) for _ in range(4))
        k_tok, v_tok = piece(3 * P), piece(3 * P)
        s_t = piece(SC)
        q_dec = piece(DEC_SEQ)
        s_new = piece(2 * RET_DV)
        sq_pair = work[:, used[0]:used[0] + 2 * T]
        sq_half = work[:, used[0] + 2 * T:used[0] + 3 * T]
        o_sq, o_std, o_rs, mix = (piece(T) for _ in range(4))
        pool_ext = piece(2 * EXT)
        assert 5 * T >= 4 * EXT
        pool_a, pool_b = (work[:, heads_only + n * EXT:heads_only + (n + 2) * EXT] for n in (0, 2))
        pooled = piece(2 * T)
        pool_rows = piece(8 * 2 * POOL_BUF)
        QE = 3 + SEQ + 3 + DEC_SEQ
        QW = QE - 3
        qk_ext = piece(2 * QE, restart=True)
        qk, qk_tanh = piece(2 * QW), piece(2 * QW)
        conv_rows = piece(16 * 2 * 3)
        g_rows = piece(2 * T + 2)
        g_mask = piece(2 * T + 2)
        g_pair = piece(T)
        g_tok = piece(3 * 64)
        num_sq, h_n, o_tanh = piece(2 * T), piece(2 * T), piece(2 * T)
        g_i, g_f, g_e, g_u, g_l, g_b = (v[:, n * T:(n + 1) * T] for v in (num_sq, h_n, o_tanh) for n in (0, 1))
        g_m = piece(8)
        late_x, dw = piece(SC), piece(SC)
        sm_t = dw
        em_b = piece(T + 2)
        iw_b, q_iw = piece(DEC_SEQ), piece(DEC_SEQ)
        n_b = piece(P)
        kw_tok = piece(3 * P)
        vm_t, vm_tok = piece(2 * T), piece(3 * ML_DV)
        c_in, c_new = piece(ML_DV), piece(2 * (ML_DV + 1))
        floor_, floor_sq, m_std, o_z = piece(T), piece(T), piece(T), piece(2 * T)
        m_rs = m_std
        GE = 2 + SEQ + 2 + DEC_SEQ
        GW = GE - 2
        g_ext = piece(2 * GE, restart=True)
        g_conv, g_act = piece(2 * GW), piece(2 * GW)
        up = piece(2 * T)
        sq_last, z = piece(2 * T), piece(KT * T)

        def two(ap, width=T):
            return ap.rearrange("p (m t) -> p m t", m=2)

        def tile(ap, t):
            return ap[:, bass.ds(t * T, T)]

        def tiles(ap, t):
            return ap[:, bass.ds(t * T, 2 * T)]

        def col(name, i=0, at=0):
            return cols[:, bass.ds(i + (COL[name] + at), 1)]

        ident, ones = con[:, CON["ident"]:CON["ident"] + P], con[:, CON["ones"]:CON["ones"] + P]
        eps, eps4 = con[:, CON["eps"]:CON["eps"] + 1], con[:, CON["eps4"]:CON["eps4"] + 1]
        late = con[:, CON["late"]:CON["late"] + SEQ]

        gb = ctx.enter_context(nc.psum_tensor("gb", [P, 4, 512], F32))
        ab = ctx.enter_context(nc.psum_tensor("ab", [P, 4, 512], F32))

        def bank(b, m):
            return gb[:, 2 * b + m, 0:T]

        def banks(b):
            return gb[:, 2 * b:2 * b + 2, 0:T]

        def both(ap):
            return ap.unsqueeze(1).to_broadcast([P, 2, T])

        def sems(text):
            return [sem(name) for name in text.split()]

        raw_loaded = [sem(f"raw_loaded{s}") for s in range(RING)]
        x_loaded = [sem(f"x_loaded{n}") for n in range(4)]
        cols_loaded, con_loaded, w_pool_loaded, ret_table_loaded, ret_s0_loaded, c_loaded = sems(
            "cols_loaded con_loaded w_pool_loaded ret_table_loaded ret_s0_loaded c_loaded")
        ret_stored, c_stored, y_stored, rows_stored = sems("ret_stored c_stored y_stored rows_stored")
        hi_ready, lo_ready, unit_used, pair_taken = sems("hi_ready lo_ready unit_used pair_taken")
        a_hi_ready, a_ready, sq_done, pool_step = sems("a_hi_ready a_ready sq_done pool_step")
        norm_sum, norm_std, rt_ready = sems("norm_sum norm_std rt_ready")
        dve_squares, last_squares, z_ready = sems("dve_squares last_squares z_ready")
        dve_step, = sems("dve_step")
        qk_ready, ret_intra, v_tok_ready, ret_state, mix_ready = sems(
            "qk_ready ret_intra v_tok_ready ret_state mix_ready")
        ret_scores, v_turned, ret_summed, ret_sq_sum = sems("ret_scores v_turned ret_summed ret_sq_sum")
        gate_tanh, ret_sq, ret_std, mix_hi = sems("gate_tanh ret_sq ret_std mix_hi")
        b_ready, = sems("b_ready")
        pooled_ready, pool_summed, pool_hi = sems("pooled_ready pool_summed pool_hi")
        conv_ready, up_ready, f_ready, gelu_ready, up_hi = sems("conv_ready up_ready f_ready gelu_ready up_hi")
        gates_dve, gates_act, gates_turned, gates_tok = sems("gates_dve gates_act gates_turned gates_tok")
        qk_conv, g_masked, late_ready, ml_intra, vm_tok_ready, ml_state, ml_var, ml_y, ml_b_ready, qk_silu = sems(
            "qk_conv g_masked late_ready ml_intra vm_tok_ready ml_state ml_var ml_y ml_b_ready qk_silu")
        m_spread, ml_scores, vm_turned, ml_summed, ml_sq_sum = sems(
            "m_spread ml_scores vm_turned ml_summed ml_sq_sum")
        qk_tanh_ready, em_ready, dw_ready, num_sq_ready, ml_std, o_tanh_ready, ml_y_hi = sems(
            "qk_tanh_ready em_ready dw_ready num_sq_ready ml_std o_tanh_ready ml_y_hi")
        y_ready, = sems("y_ready")

        def ffn_blocks(unit0, pair0):
            out, f = [], 0
            for k in BLOCKS:
                down_unit, down_pair = unit0 + 4 * k, pair0 + k
                out.append((f, k, unit0, pair0, down_unit, down_pair))
                unit0, pair0, f = down_unit + KT // UM * (k // UK), down_pair + KT // UM, f + k
            return out

        block = ctx.enter_context(nc.Block())

        @block.sync
        def _(sp):
            def load(u):
                if u.i is not None or u.first >= RING:
                    sp.wait_ge(lo_ready, u.number(1 - RING))
                sp.dma_start(raw[:, u.slot * UW:(u.slot + 1) * UW],
                             weights[bass.ds(u.number(), 1)].rearrange("o p n -> p (o n)"))\
                    .then_inc(raw_loaded[u.slot], 16)

            def loads(first, count):
                with sp.Fori(0, count // RING) as i:
                    for j in range(RING):
                        load(Unit(first + j, i, RING))

            def head_row(array, h):
                return array[bass.ds(h, 1)].rearrange("o p n -> p (o n)")

            for n in range(4):
                q = slice(n * 4 * T, (n + 1) * 4 * T)
                sp.dma_start(x[:, q], x_in[:, q]).then_inc(x_loaded[n], 16)
                if n == 0:
                    sp.dma_start(cols[:], cols_in).then_inc(cols_loaded, 16)
                load(Unit(n))
            sp.dma_start(con[:], consts_in).then_inc(con_loaded, 16)
            sp.dma_start(ret_table, ret_tables_in[0]).then_inc(ret_table_loaded, 16)
            sp.dma_start(ret_s0, ret_state_in[0]).then_inc(ret_s0_loaded, 16)
            sp.dma_start(w_pool, w_pool_in).then_inc(w_pool_loaded, 16)
            for j in range(4, 16):
                load(Unit(j))
            with sp.Fori(1, HEADS) as h:
                for j in range(4):
                    load(Unit(8 + j, h, 8))
                sp.wait_ge(ret_intra, h)
                sp.dma_start(ret_table, head_row(ret_tables_in, h)).then_inc(ret_table_loaded, 16)
                for j in range(4, 8):
                    load(Unit(8 + j, h, 8))
                sp.wait_ge(ret_state, h)
                sp.dma_start(head_row(ret_out, h - 1), s_new).then_inc(ret_stored, 16)
                sp.dma_start(ret_s0, head_row(ret_state_in, h)).then_inc(ret_s0_loaded, 16)
            first = U_HEADS + HEADS * 8 + 8
            loads(first, 8)
            sp.wait_ge(ret_state, HEADS)
            sp.dma_start(ret_out[HEADS - 1], s_new).then_inc(ret_stored, 16)
            loads(first + 8, U_FFN0 + 32 - first - 8)
            sp.wait_ge(b_ready, 2 * HEADS)
            sp.dma_start(pool_out, pool_rows).then_inc(rows_stored, 16)
            loads(U_FFN0 + 32, U_ML - U_FFN0 - 32)
            for j in range(12):
                load(Unit(U_ML + j))
            sp.dma_start(c_in, ml_state_in[0]).then_inc(c_loaded, 16)
            with sp.Fori(1, HEADS) as h:
                for j in range(12):
                    load(Unit(U_ML + j, h, 12))
                sp.wait_ge(ml_state, h)
                sp.dma_start(head_row(c_out, h - 1), c_new).then_inc(c_stored, 16)
                sp.dma_start(c_in, head_row(ml_state_in, h)).then_inc(c_loaded, 16)
            loads(U_OUTC, 12)
            sp.wait_ge(ml_state, HEADS)
            sp.dma_start(c_out[HEADS - 1], c_new).then_inc(c_stored, 16)
            sp.dma_start(conv_out, conv_rows).then_inc(rows_stored, 16)
            sp.dma_start(m_out, g_m[0:HEADS, 0:2]).then_inc(rows_stored, 16)
            loads(U_OUTC + 12, UNITS - U_OUTC - 12)
            sp.wait_ge(f_ready, FT)
            sp.dma_start(ffn_out, ffn_rows[:]).then_inc(rows_stored, 16)
            for g in range(4):
                sp.wait_ge(y_ready, g + 1)
                sp.dma_start(y_out[:, g * 4 * T:(g + 1) * 4 * T], z[:, g * 4 * T:(g + 1) * 4 * T])\
                    .then_inc(y_stored, 16)
            sp.wait_ge(ret_stored, 16 * HEADS)
            sp.wait_ge(c_stored, 16 * HEADS)
            sp.wait_ge(rows_stored, 16 * 4)
            sp.wait_ge(y_stored, 16 * 4)

        @block.gpsimd
        def _(pool):
            step = Count(pool_step)

            def add_square(t, sem_, at):
                pool.wait_ge(pool_step, step.value())
                pool.wait_ge(sem_, at)
                pool.wait_ge(cols_loaded, 16)
                step.inc(nc.gpsimd.tensor_tensor(sq_one[:], tile(x, t), tile(x, t), ALU.mult))
                pool.wait_ge(pool_step, step.value())
                step.inc(nc.gpsimd.tensor_tensor(sq_sum[:], sq_sum[:], sq_one[:], ALU.add))

            def squares(norm, pair, pairs=KT // 2, loaded=False):
                if norm:
                    pool.wait_ge(norm_sum, norm)
                step.inc(nc.gpsimd.memset(sq_sum[:], 0.0))
                with counted(pool, pairs, [(step, 4)]) as i:
                    for m in range(2):
                        if loaded:
                            add_square(i * 2 + m, cols_loaded, 16)
                        else:
                            add_square(i * 2 + m, pair_taken, i + (pair + 1))
                pool.wait_ge(pool_step, step.value())
                nc.gpsimd.tensor_copy(sq_one[:, 0:1], sq_sum[:, 0:1]).then_inc(sq_done, 1)

            pool.wait_ge(x_loaded[0], 16)
            pool.wait_ge(x_loaded[1], 16)
            squares(0, 0, KT // 4, loaded=True)
            squares(1, PR_OUTA)
            squares(2, PR_GATES - KT // 2)
            squares(3, PR_OUTC)
            squares(4, PR_END - KT // 2, KT // 2 - 1)

        @block.tensor
        def _(pe):
            def unit(u, kg, groups, hi, lo, b, taken=None, outs=UM):
                pe.wait_ge(lo_ready, u.number(1))
                if kg == 0 and taken is not None:
                    pe.wait_ge(pair_taken, taken)
                for m in range(outs):
                    for k in range(UK):
                        at = u.slot * UW + (k * outs + m) * P
                        t = (kg * UK + k) * T
                        for n, (w, v) in enumerate(((w_hi, hi), (w_hi, lo), (w_lo, hi))):
                            last = nc.tensor.matmul(bank(b, m), w[:, at:at + P], v[:, t:t + T],
                                                    start=kg == k == n == 0,
                                                    stop=kg == groups - 1 and k == UK - 1 and n == 2)
                last.then_inc(unit_used, 1)

            def small(out, lhs, rhs, start=True, stop=True):
                return nc.tensor.matmul(out, lhs, rhs, start=start, stop=stop)

            def norm(k, more=((con_loaded, 16),)):
                pe.wait_ge(sq_done, k + 1)
                pe.wait_ge(*more[0])
                parts = [sq_sum[:], *more[1:]]
                for n, part in enumerate(parts):
                    last = small(ab[:, 0, 0:T], ones, part, start=n == 0, stop=n == len(parts) - 1)
                last.then_inc(norm_sum, 1)

            def turn(out, src, width, parts=P):
                return nc.tensor.transpose(out, src, ident[0:parts, 0:parts])

            def ret_scores_of(h):
                pe.wait_ge(qk_ready, h + 1)
                for n in range(3):
                    w = P if n < 2 else DEC_SEQ
                    turn(ab[0:w, 0, n * P:(n + 1) * P], k_t[:, n * P:n * P + w], w)
                small(ab[:, 2, 0:SEQ], k_t[:, 0:P], q_t[:, 0:SEQ])
                small(ab[:, 2, SEQ:SEQ + P], k_t[:, P:SEQ], q_t[:, P:SEQ])
                small(ab[0:DEC_SEQ, 2, SEQ + P:SC], k_t[:, SEQ:T], q_t[:, SEQ:T]).then_inc(ret_scores, 1)

            def ret_turn_v(h):
                pe.wait_ge(pair_taken, h * 2 + 2)
                for n in range(3):
                    w = P if n < 2 else DEC_SEQ
                    last = turn(ab[0:w, 1, n * P:(n + 1) * P], v_t[:, n * P:n * P + w], w)
                last.then_inc(v_turned, 1)

            def ret_sums(h):
                pe.wait_ge(v_tok_ready, h + 1)
                pe.wait_ge(ret_intra, h + 1)
                pe.wait_ge(ret_s0_loaded, h * 16 + 16)
                small(ab[:, 3, 0:SEQ], v_tok[:, 0:P], s_t[:, 0:SEQ], stop=False)
                small(ab[:, 3, P:SEQ], v_tok[:, P:2 * P], s_t[:, SEQ:SEQ + P], start=False)
                small(ab[:, 3, SEQ:T], v_tok[0:DEC_SEQ, 2 * P:3 * P], s_t[0:DEC_SEQ, SEQ + P:SC], stop=False)
                small(ab[:, 3, SEQ:T], ret_s0, q_dec, start=False)
                small(ab[:, 0, 0:P], k_tok[:, 0:P], v_tok[:, 0:P], stop=False)
                small(ab[:, 0, 0:P], k_tok[:, P:2 * P], v_tok[:, P:2 * P], start=False)
                small(ab[:, 0, P:2 * P], k_tok[0:DEC_SEQ, 2 * P:3 * P], v_tok[0:DEC_SEQ, 2 * P:3 * P])\
                    .then_inc(ret_summed, 1)

            def ret_square_sum(h):
                pe.wait_ge(ret_sq, h + 1)
                small(ab[:, 1, 0:T], ones, o_sq).then_inc(ret_sq_sum, 1)

            def pool_product(j):
                pe.wait_ge(pooled_ready, j + 1)
                pe.wait_ge(b_ready, HEADS + 2 * j)
                for m in range(2):
                    for c in range(2):
                        at = (2 * (POOL_GROUPS - 1 - j) + c) * 2 * P + m * P
                        last = small(ab[:, 2 + m, 0:T], w_pool[:, at:at + P], pooled[:, c * T:(c + 1) * T],
                                     start=c == 0, stop=c == 1)
                last.then_inc(pool_summed, 1)

            def ret_tail(h, j):
                if j == 1:
                    ret_turn_v(h)
                if j == 2:
                    ret_sums(h)
                if j == 4:
                    ret_square_sum(h)

            def head(h, i, tail):
                for j in range(8):
                    q, kg = divmod(j, 4)
                    if kg == 0 and i is None:
                        taken = None
                    elif kg == 0:
                        taken = i * 2 + (q + 1)
                    if i is None and kg == j:
                        pe.wait_ge(a_ready, 2 * kg + 2)
                    unit(Unit(j) if i is None else Unit(8 + j, i, 8), kg, 4, a_hi, a_lo, q,
                         taken if kg == 0 else None)
                    if i is None and j == 2:
                        norm(0, ((dve_squares, 1), sq_half))
                    if tail:
                        ret_tail(h - 1, j)
                    if j == 6:
                        ret_scores_of(h)

            head(0, None, False)
            with pe.Fori(0, HEADS - 1) as i:
                head(i + 1, i, True)
            pe.wait_ge(w_pool_loaded, 16)
            for p in range(POOL_GROUPS):
                for kg in range(4):
                    j = 4 * p + kg
                    unit(Unit(U_POOL + j), kg, 4, a_hi, a_lo, p % 2, PR_POOL + p - 1)
                    ret_tail(HEADS - 1, j)
                    if j in (7, 10, 14):
                        pool_product((7, 10, 14).index(j))

            def out_pairs(unit0, pair0, after_step, before_step):
                for kg in range(4):
                    before_step(kg)
                    unit(Unit(unit0 + kg), kg, 4, b_hi, b_lo, 0, pair0 - 1)
                    after_step(kg)
                for kg in range(4):
                    unit(Unit(unit0 + 4 + kg), kg, 4, b_hi, b_lo, 1, pair0)
                with pe.Fori(0, KT // UM // 2 - 1) as i:
                    for p in range(2):
                        for kg in range(4):
                            unit(Unit(unit0 + 8 + 4 * p + kg, i, 8), kg, 4, b_hi, b_lo, p, i * 2 + (pair0 + 1 + p))

            def after_a(kg):
                if kg == 1:
                    pool_product(3)

            def before_a(kg):
                pe.wait_ge(b_ready, 4 * kg + 4)

            out_pairs(U_OUTA, PR_OUTA, after_a, before_a)

            def ffn(unit0, pair0, k_norm, a_base, f_base):
                for b, (f, k, u0, p0, down_u, down_p) in enumerate(ffn_blocks(unit0, pair0)):
                    done = 0
                    if b == 0:
                        for j in range(8):
                            if j < 4:
                                pe.wait_ge(a_ready, a_base + 2 * j + 2)
                            unit(Unit(u0 + j), j % 4, 4, a_hi, a_lo, j // 4, p0 + j // 4 - 1)
                            if j == 1:
                                norm(k_norm)
                        done = 1
                    with pe.Fori(0, k // 2 - done) as i:
                        for j in range(8):
                            unit(Unit(u0 + 8 * done + j, i, 8), j % 4, 4, a_hi, a_lo, j // 4,
                                 i * 2 + (p0 + 2 * done + j // 4 - 1))
                    groups = k // UK
                    for kg in range(groups):
                        pe.wait_ge(f_ready, f_base + f // 2 + 2 * kg + 2)
                        unit(Unit(down_u + kg), kg, groups, b_hi, b_lo, 0, down_p - 1)
                    if groups == 4:
                        for kg in range(4):
                            unit(Unit(down_u + 4 + kg), kg, groups, b_hi, b_lo, 1, down_p)
                        with pe.Fori(0, 3) as i:
                            for p in range(2):
                                for kg in range(4):
                                    unit(Unit(down_u + 8 + 4 * p + kg, i, 8), kg, groups, b_hi, b_lo, p,
                                         i * 2 + (down_p + 1 + p))
                    else:
                        for p in range(1, KT // UM):
                            for kg in range(groups):
                                unit(Unit(down_u + groups * p + kg), kg, groups, b_hi, b_lo, p % 2, down_p + p - 1)

            ffn(U_FFN0, PR_FFN0, 1, 8, 0)

            for kg in range(4):
                pe.wait_ge(a_ready, 16 + 2 * kg + 2)
                unit(Unit(U_GATES + kg), kg, 4, a_hi, a_lo, 0, PR_GATES - 1, outs=1)

            def spread(h):
                pe.wait_ge(g_masked, h + 1)
                small(ab[:, 0, 0:T], ones[0:HEADS, :], g_mask[0:HEADS, 0:T])
                small(ab[:, 1, 0:T + 2], ones[0:HEADS, :], g_mask[0:HEADS, T:2 * T + 2]).then_inc(m_spread, 1)

            def ml_scores_of(h):
                pe.wait_ge(qk_silu, h + 1)
                q, k = qk[:, 0:QW], qk[:, QW:2 * QW]
                s = SEQ + 3
                for n, (at, w) in enumerate(((0, P), (P, P), (s, DEC_SEQ))):
                    turn(ab[0:w, 3, n * P:(n + 1) * P], k[:, at:at + w], w)
                small(ab[:, 2, 0:SEQ], k[:, 0:P], q[:, 0:SEQ])
                small(ab[:, 2, SEQ:SEQ + P], k[:, P:SEQ], q[:, P:SEQ])
                small(ab[0:DEC_SEQ, 2, SEQ + P:SC], k[:, s:s + DEC_SEQ], q[:, s:s + DEC_SEQ]).then_inc(ml_scores, 1)

            def ml_turn_v(h):
                pe.wait_ge(pair_taken, h * 3 + (PR_ML + 2))
                pe.wait_ge(em_ready, h * 2 + 2)
                for e in range(2):
                    for n in range(3):
                        w = P if n < 2 else DEC_SEQ
                        out = ab[0:w, 0, n * ML_DV + e * P:n * ML_DV + (e + 1) * P] if n < 2 else \
                            ab[0:w, 1, e * P:(e + 1) * P]
                        last = turn(out, vm_t[:, e * T + n * P:e * T + n * P + w], w)
                last.then_inc(vm_turned, 1)

            def ml_sums(h):
                pe.wait_ge(vm_tok_ready, h + 1)
                pe.wait_ge(ml_intra, h + 1)
                pe.wait_ge(c_loaded, h * 16 + 16)

                def v(n, e):
                    return vm_tok[:, n * ML_DV + e * P:n * ML_DV + (e + 1) * P]

                for e in range(3):
                    out = ab[:, e, :]
                    v0, v1, v2, s0 = (v(0, e), v(1, e), v(2, e)[0:DEC_SEQ], c_in[:, e * P:(e + 1) * P]) if e < 2 \
                        else (ones, ones, ones[0:DEC_SEQ, :], n_b)
                    small(out[:, 0:SEQ], v0, sm_t[:, 0:SEQ], stop=False)
                    small(out[:, P:SEQ], v1, sm_t[:, SEQ:SEQ + P], start=False)
                    small(out[:, SEQ:T], v2, sm_t[0:DEC_SEQ, SEQ + P:SC], stop=False)
                    small(out[:, SEQ:T], s0, q_iw, start=False)
                k0, k1, k2 = kw_tok[:, 0:P], kw_tok[:, P:2 * P], kw_tok[0:DEC_SEQ, 2 * P:3 * P]
                small(ab[:, 3, 0:ML_DV], k0, vm_tok[:, 0:ML_DV], stop=False)
                small(ab[:, 3, 0:ML_DV], k1, vm_tok[:, ML_DV:2 * ML_DV], start=False)
                small(ab[:, 3, ML_DV:2 * ML_DV], k2, vm_tok[0:DEC_SEQ, 2 * ML_DV:3 * ML_DV])
                small(ab[:, 2, T:T + 1], k0, ones[:, 0:1], stop=False)
                small(ab[:, 2, T:T + 1], k1, ones[:, 0:1], start=False)
                small(ab[:, 2, T + 1:T + 2], k2, ones[0:DEC_SEQ, 0:1]).then_inc(ml_summed, 1)

            def ml_square_sum(h):
                pe.wait_ge(ml_state, h + 1)
                small(ab[:, 2, 0:T], ones, num_sq[:, 0:T]).then_inc(ml_sq_sum, 1)

            def ml_head(h, i):
                for j in range(12):
                    q, kg = divmod(j, 4)
                    u = Unit(U_ML + j) if i is None else Unit(U_ML + 12 + j, i, 12)
                    taken = PR_ML + q - (q > 0) if i is None else i * 3 + (PR_ML + 3 + q - (q > 0))
                    if i is None and q == 0:
                        taken = PR_GATES
                    unit(u, kg, 4, a_hi, a_lo, (1, 0, 1)[q], taken)
                    if i is None and j == 0:
                        norm(2)
                    if i is None and j == 5:
                        pe.wait_ge(gates_act, 4)
                        for n in range(3):
                            w = P if n < 2 else DEC_SEQ
                            last = turn(ab[0:w, 3, n * 64:(n + 1) * 64], g_pair[0:64, n * P:n * P + w], w, 64)
                        last.then_inc(gates_turned, 1)
                    if j == (3 if i is not None else 6):
                        spread(h)
                    if j == (6 if i is not None else 7):
                        ml_scores_of(h)
                    if j == 8:
                        ml_turn_v(h)
                    if j == 9:
                        ml_sums(h)
                    if j == 10:
                        ml_square_sum(h)

            ml_head(0, None)
            with pe.Fori(0, HEADS - 1) as i:
                ml_head(i + 1, i)

            def before_c(kg):
                pe.wait_ge(ml_b_ready, 2 * kg + 2)

            out_pairs(U_OUTC, PR_OUTC, lambda kg: None, before_c)
            ffn(U_FFN1, PR_FFN1, 3, 24, FT // 2)
            norm(4, ((last_squares, 1), sq_last[:, 0:T], sq_last[:, T:2 * T]))

        @block.scalar
        def _(act):
            def split(u):
                if not u.exists:
                    return
                act.wait_ge(raw_loaded[u.slot], u.turn(16, 16))
                if u.i is not None or u.first >= RING:
                    act.wait_ge(unit_used, u.number(1 - RING))
                at = u.slot * UW
                nc.scalar.activation(w_hi[:, at:at + UW], raw[:, at:at + UW], ACT.Copy).then_inc(hi_ready, 1)

            def a_upper(p, weight, sem_, at):
                act.wait_ge(sem_, at)
                act.wait_ge(cols_loaded, 16)
                for m in range(2):
                    last = nc.scalar.activation(tile(a_hi, p * 2 + m), tile(x, p * 2 + m), ACT.Copy,
                                                scale=col(weight, p * 2, m))
                last.then_inc(a_hi_ready, 1)

            def norm(k):
                act.wait_ge(norm_sum, k + 1)
                nc.scalar.activation(std[:], ab[:, 0, 0:T], ACT.Sqrt, scale=1.0 / D_MODEL, bias=eps)\
                    .then_inc(norm_std, 1)

            def ret_tail(h, j):
                if j == 1:
                    act.wait_ge(pair_taken, h * 2 + 2)
                    nc.scalar.activation(tanh_g, z_g, ACT.Tanh, scale=0.5).then_inc(gate_tanh, 1)
                if j == 4:
                    act.wait_ge(ret_summed, h + 1)
                    nc.scalar.activation(mix, ab[:, 3, 0:T], ACT.Copy)
                    nc.scalar.activation(o_sq, ab[:, 3, 0:T], ACT.Square).then_inc(ret_sq, 1)
                if j == 5:
                    act.wait_ge(ret_sq_sum, h + 1)
                    nc.scalar.activation(o_std, ab[:, 1, 0:T], ACT.Sqrt, scale=4.0 / RET_DV, bias=eps4)\
                        .then_inc(ret_std, 1)
                if j == 7:
                    act.wait_ge(mix_ready, h + 1)
                    act.wait_ge(cols_loaded, 16)
                    nc.scalar.activation(tile(b_hi, h), mix, ACT.Copy).then_inc(mix_hi, 1)

            def pool_upper(j):
                act.wait_ge(pool_summed, j + 1)
                for m in range(2):
                    last = nc.scalar.activation(tile(b_hi, HEADS + 2 * j + m), ab[:, 2 + m, 0:T], ACT.Copy,
                                                scale=col("pool_scale", 0, 2 * (POOL_GROUPS - 1 - j) + m))
                last.then_inc(pool_hi, 1)

            act.wait_ge(cols_loaded, 16)
            for s in range(AHEAD):
                if s == 0:
                    split(Unit(s))
                for p in range(2):
                    a_upper(2 * s + p, "mix0", x_loaded[s], 16)
                if s:
                    split(Unit(s))
            a_upper(6, "mix0", x_loaded[3], 16)
            a_upper(7, "mix0", x_loaded[3], 16)
            for j in range(8):
                split(Unit(AHEAD + j))
                if j == 2:
                    act.wait_ge(con_loaded, 16)
                    norm(0)
            with act.Fori(0, HEADS - 1) as i:
                for j in range(8):
                    split(Unit(8 + AHEAD + j, i, 8))
                    ret_tail(i, j)
            for j in range(16):
                split(Unit(U_POOL + AHEAD + j))
                ret_tail(HEADS - 1, j)
                if j in (8, 11, 15):
                    pool_upper((8, 11, 15).index(j))

            def out_pairs(unit0, pair0, weight, extra):
                for kg in range(4):
                    split(Unit(unit0 + AHEAD + kg))
                    extra(kg)
                with act.Fori(0, KT // UM - 1) as i:
                    for kg in range(4):
                        split(Unit(unit0 + AHEAD + 4 + kg, i, 4))
                        if kg == 1:
                            a_upper(i, weight, pair_taken, i + (pair0 + 1))

            def extra_a(kg):
                if kg == 2:
                    pool_upper(3)

            out_pairs(U_OUTA, PR_OUTA, "ffn0", extra_a)

            def ffn_gelu(g):
                act.wait_ge(conv_ready, g + 1)
                nc.scalar.activation(g_act, g_conv, ACT.Gelu_apprx_tanh).then_inc(gelu_ready, 1)

            def ffn_upper(g, t):
                act.wait_ge(up_ready, g + 1)
                act.wait_ge(cols_loaded, 16)
                nc.scalar.activation(tiles(b_hi, t), up, ACT.Copy).then_inc(up_hi, 1)

            def z_of(p):
                for m in range(2):
                    last = nc.scalar.activation(tile(z, p * 2 + m), tile(x, p * 2 + m), ACT.Copy,
                                                scale=col("final", p * 2, m))
                last.then_inc(z_ready, 1)

            def ffn(unit0, pair0, k_norm, g0, weight, next_weight):
                for b, (f, k, u0, p0, down_u, down_p) in enumerate(ffn_blocks(unit0, pair0)):
                    g = g0 + f // 2
                    for j in range(8):
                        split(Unit(u0 + AHEAD + j))
                        if j == 1 and b == 0:
                            a_upper(KT // UM - 1, weight, pair_taken, p0)
                        if j == 2 and b == 0:
                            norm(k_norm)
                        if j == 6:
                            ffn_gelu(g)
                    with act.Fori(0, k // 2 - 1) as i:
                        for j in range(8):
                            split(Unit(u0 + AHEAD + 8 + j, i, 8))
                            if j == 1:
                                ffn_upper(i + g, i * 2)
                            if j == 6:
                                ffn_gelu(i + (g + 1))
                    groups = k // UK
                    final = b == len(BLOCKS) - 1
                    for kg in range(groups):
                        split(Unit(down_u + AHEAD + kg))
                        if kg == 0:
                            ffn_upper(g + k // 2 - 1, k - 2)
                    if groups == 4:
                        assert not final
                        with act.Fori(0, KT // UM - 1) as i:
                            for kg in range(4):
                                split(Unit(down_u + AHEAD + 4 + kg, i, 4))
                    else:
                        for p in range(1, KT // UM):
                            for kg in range(groups):
                                split(Unit(down_u + AHEAD + groups * p + kg))
                                if kg == 1 and next_weight:
                                    a_upper(p - 1, next_weight, pair_taken, down_p + p)
                                elif kg == 1:
                                    act.wait_ge(pair_taken, down_p + p)
                                    z_of(p - 1)

            ffn(U_FFN0, PR_FFN0, 1, 0, "ffn0", "mix1")

            for kg in range(4):
                split(Unit(U_GATES + AHEAD + kg))
                if kg == 0:
                    a_upper(KT // UM - 1, "mix1", pair_taken, PR_GATES)

            H8 = slice(0, HEADS)

            def gates(j):
                if j == 0:
                    act.wait_ge(gates_dve, 1)
                    nc.scalar.activation(g_u[H8, :], g_e[H8, :], ACT.Exp, scale=-1.0).then_inc(gates_act, 1)
                if j == 1:
                    act.wait_ge(gates_dve, 2)
                    nc.scalar.activation(g_l[H8, :], g_b[H8, :], ACT.Ln).then_inc(gates_act, 1)
                if j == 2:
                    act.wait_ge(gates_dve, 3)
                    nc.scalar.activation(g_rows[H8, T:2 * T], g_e[H8, :], ACT.Exp, scale=-1.0)
                    nc.scalar.activation(g_rows[H8, 2 * T:2 * T + 1], cols[H8, COL["m0"]:COL["m0"] + 1], ACT.Exp,
                                         bias=g_m[H8, 3:4]).then_inc(gates_act, 1)
                    nc.scalar.activation(g_pair[32:32 + HEADS, 0:SEQ], g_pair[H8, 0:SEQ], ACT.Exp,
                                         bias=g_m[H8, 2:3])
                    nc.scalar.activation(g_pair[32:32 + HEADS, SEQ:T], g_pair[H8, SEQ:T], ACT.Exp,
                                         bias=g_m[H8, 3:4]).then_inc(gates_act, 1)

            def ml_tail(h, j):
                if j == 0:
                    act.wait_ge(pair_taken, h * 3 + (PR_ML + 3))
                    nc.scalar.activation(o_tanh, o_z, ACT.Tanh, scale=0.5).then_inc(o_tanh_ready, 1)
                if j == 2:
                    act.wait_ge(ml_y, h + 1)
                    act.wait_ge(cols_loaded, 16)
                    nc.scalar.activation(tiles(b_hi, h * 2), o_z, ACT.Copy).then_inc(ml_y_hi, 1)

            def ml_steps(h, j, first=False):
                if j == 5:
                    act.wait_ge(qk_conv, h + 1)
                    nc.scalar.activation(qk_tanh, qk, ACT.Tanh, scale=0.5).then_inc(qk_tanh_ready, 1)
                if j == (6 if not first else 7):
                    act.wait_ge(m_spread, h + 1)
                    nc.scalar.activation(em_b, ab[:, 1, 0:T + 2], ACT.Copy).then_inc(em_ready, 1)
                    act.wait_ge(em_ready, h * 2 + 1)
                    act.wait_ge(late_ready, h + 1)
                    nc.scalar.activation(iw_b, ab[:, 0, SEQ:T], ACT.Exp, scale=-1.0, bias=em_b[:, T + 1:T + 2])\
                        .then_inc(em_ready, 1)
                    nc.scalar.activation(dw[:, 0:SEQ + P], late_x[:, 0:SEQ + P], ACT.Exp, scale=-1.0)
                    nc.scalar.activation(dw[0:DEC_SEQ, SEQ + P:SC], late_x[0:DEC_SEQ, SEQ + P:SC], ACT.Exp,
                                         scale=-1.0).then_inc(dw_ready, 1)
                if j == 10:
                    act.wait_ge(ml_summed, h + 1)
                    nc.scalar.activation(two(num_sq), ab[:, 0:2, 0:T], ACT.Square)
                    nc.scalar.activation(floor_, ab[:, 2, 0:T], ACT.Abs).then_inc(num_sq_ready, 1)
                if j == 11:
                    act.wait_ge(ml_var, h + 1)
                    nc.scalar.activation(m_std, m_std, ACT.Sqrt, scale=4.0).then_inc(ml_std, 1)

            for j in range(12):
                split(Unit(U_ML + AHEAD + j))
                if j == 1:
                    norm(2)
                gates(j - 2)
                ml_steps(0, j, first=True)
            with act.Fori(0, HEADS - 1) as i:
                for j in range(12):
                    split(Unit(U_ML + AHEAD + 12 + j, i, 12))
                    ml_tail(i, j)
                    ml_steps(i + 1, j)
            out_pairs(U_OUTC, PR_OUTC, "ffn1", lambda kg: ml_tail(HEADS - 1, kg))
            ffn(U_FFN1, PR_FFN1, 3, FT // 2, "ffn1", None)
            act.wait_ge(pair_taken, PR_END)
            nc.scalar.activation(sq_last, tiles(x, KT - 2), ACT.Square).then_inc(last_squares, 1)
            z_of(KT // UM - 1)
            norm(4)

        @block.vector
        def _(dve):
            step = Count(dve_step)
            V = nc.vector

            def own():
                dve.wait_ge(dve_step, step.value())

            def split(u):
                if not u.exists:
                    return
                dve.wait_ge(hi_ready, u.number(1))
                at = u.slot * UW
                V.tensor_tensor(w_lo[:, at:at + UW], raw[:, at:at + UW], w_hi[:, at:at + UW].bitcast(F32),
                                ALU.subtract).then_inc(lo_ready, 1)

            def a_lower(p, weight, ready):
                dve.wait_ge(a_hi_ready, ready)
                for m in range(2):
                    t = p * 2 + m
                    last = V.scalar_tensor_tensor(tile(a_lo, t), tile(x, t), col(weight, p * 2, m),
                                                  tile(a_hi, t).bitcast(F32), ALU.mult, ALU.subtract)
                last.then_inc(a_ready, 1)

            def norm(k):
                dve.wait_ge(norm_std, k + 1)
                V.reciprocal(rt[:], std[:]).then_inc(rt_ready, 1)
                dve.wait_ge(rt_ready, k + 1)

            def used(u_last):
                dve.wait_ge(unit_used, u_last)

            def add_to_x(p, b, units, taken):
                used(units)
                V.tensor_tensor(two(tiles(x, p * 2)), banks(b), two(tiles(x, p * 2)), ALU.add)\
                    .then_inc(pair_taken, 1)
                dve.wait_ge(pair_taken, taken)

            half = slice(0, P // 2), slice(P // 2, P)

            def ret_qk(h, units):
                used(units)
                for dst, swap, m in ((q_t, q_swap, 0), (k_t, k_swap, 1)):
                    V.tensor_tensor(dst, bank(0, m), cos_r, ALU.mult)
                    V.tensor_tensor(swap[half[0], :], bank(0, m)[half[1], :], sin_r[half[1], :], ALU.mult)
                    last = V.tensor_tensor(swap[half[1], :], bank(0, m)[half[0], :], sin_r[half[0], :], ALU.mult)
                last.then_inc(pair_taken, 1)
                dve.wait_ge(pair_taken, h * 2 + 1)
                V.tensor_tensor(q_t, q_t, q_swap, ALU.add)
                V.tensor_tensor(k_t, k_t, k_swap, ALU.add).then_inc(qk_ready, 1)
                dve.wait_ge(qk_ready, h + 1)

            def ret_weigh(h):
                dve.wait_ge(ret_table_loaded, h * 16 + 16)
                dve.wait_ge(ret_scores, h + 1)
                s = ab[:, 2, :]
                V.tensor_tensor(s_t[:, 0:SEQ], s[:, 0:SEQ], ret_table[:, 0:SEQ], ALU.mult)
                V.tensor_tensor(s_t[:, SEQ:SEQ + P], s[:, SEQ:SEQ + P], ret_table[:, 0:P], ALU.mult)
                V.tensor_tensor(s_t[0:DEC_SEQ, SEQ + P:SC], s[0:DEC_SEQ, SEQ + P:SC],
                                ret_table[0:DEC_SEQ, 0:DEC_SEQ], ALU.mult)
                for n in range(3):
                    w = P if n < 2 else DEC_SEQ
                    V.tensor_scalar(k_tok[0:w, n * P:(n + 1) * P], ab[0:w, 0, n * P:(n + 1) * P],
                                    con[0:w, bass.ds(h + (CON["kdec"] + n * HEADS), 1)], None, ALU.mult)
                V.tensor_tensor(q_dec, q_t[:, SEQ:T], ret_table[:, SEQ:RET_TABLE], ALU.mult).then_inc(ret_intra, 1)

            def ret_tail(h, j, stored=True):
                if j == 0:
                    used(h * 8 + 8)
                    V.tensor_tensor(v_t, bank(1, 0), rt[:], ALU.mult)
                    V.tensor_tensor(z_g, bank(1, 1), rt[:], ALU.mult).then_inc(pair_taken, 1)
                if j == 2:
                    dve.wait_ge(gate_tanh, h + 1)
                    dve.wait_ge(pair_taken, h * 2 + 2)
                    V.scalar_tensor_tensor(gate, tanh_g, 1.0, z_g, ALU.add, ALU.mult)
                    dve.wait_ge(v_turned, h + 1)
                    V.tensor_copy(v_tok[:, 0:2 * P], ab[:, 1, 0:2 * P])
                    V.tensor_copy(v_tok[0:DEC_SEQ, 2 * P:3 * P], ab[0:DEC_SEQ, 1, 2 * P:3 * P])\
                        .then_inc(v_tok_ready, 1)
                if j == 3:
                    dve.wait_ge(ret_summed, h + 1)
                    if stored:
                        dve.wait_ge(ret_stored, h * 16)
                    V.tensor_copy(s_new[:, 0:RET_DV], ab[:, 0, 0:P])
                    V.scalar_tensor_tensor(s_new[:, RET_DV:2 * RET_DV], ret_s0,
                                           con[:, bass.ds(h + CON["gamma_l"], 1)], ab[:, 0, P:2 * P],
                                           ALU.mult, ALU.add).then_inc(ret_state, 1)
                if j == 6:
                    dve.wait_ge(v_tok_ready, h + 1)
                    dve.wait_ge(ret_std, h + 1)
                    step.inc(V.tensor_tensor(mix, mix, gate, ALU.mult))
                    step.inc(V.reciprocal(o_rs, o_std))
                    own()
                    V.tensor_tensor(mix, mix, o_rs, ALU.mult).then_inc(mix_ready, 1)
                if j == 7:
                    dve.wait_ge(mix_ready, h + 1)
                    dve.wait_ge(mix_hi, h + 1)
                    V.tensor_tensor(tile(b_lo, h), mix, tile(b_hi, h).bitcast(F32), ALU.subtract)\
                        .then_inc(b_ready, 1)

            def pool_steps(j, units):
                used(units)
                if j:
                    dve.wait_ge(pool_summed, j)
                taken, b = PR_POOL + j + 1, j % 2
                j = POOL_GROUPS - 1 - j
                ext, dst, other = two(pool_ext, EXT), two(pool_a, EXT), two(pool_b, EXT)
                s0 = POOL_BUF + SEQ + POOL_BUF
                src = banks(b)
                V.tensor_copy(ext[:, :, POOL_BUF + SEQ:s0],
                              cols[:, COL["pool_hist"] + 2 * j * POOL_BUF:COL["pool_hist"] + 2 * (j + 1) * POOL_BUF]
                              .rearrange("p (m t) -> p m t", m=2))
                V.tensor_tensor(ext[:, :, POOL_BUF:POOL_BUF + SEQ], src[:, :, 0:SEQ], both(rt[:])[:, :, 0:SEQ],
                                ALU.mult)
                V.tensor_tensor(ext[:, :, s0:EXT], src[:, :, SEQ:T], both(rt[:])[:, :, SEQ:T], ALU.mult)\
                    .then_inc(pair_taken, 1)
                dve.wait_ge(pair_taken, taken)
                rows = pool_rows[:, 4 * j * POOL_BUF:4 * (j + 1) * POOL_BUF]\
                    .rearrange("p (m g t) -> p m g t", m=2, g=2)
                V.tensor_copy(rows[:, :, 0, :], ext[:, :, SEQ:SEQ + POOL_BUF])
                V.tensor_copy(rows[:, :, 1, :], ext[:, :, EXT - POOL_BUF:EXT])
                src, width = ext, EXT
                for level in range(j + 1):
                    shift = 1 << level
                    width -= shift
                    step.inc(V.tensor_tensor(dst[:, :, 0:width], src[:, :, shift:shift + width],
                                             src[:, :, 0:width], ALU.add))
                    own()
                    src, dst, other = dst, other, dst
                w = 2 << j
                p0, d0 = POOL_BUF - w + 1, s0 - w + 1
                fix = con[:, CON["pool_fix"] + 16 * j:CON["pool_fix"] + 16 * (j + 1)]
                step.inc(V.tensor_tensor(src[:, :, p0:p0 + 16], src[:, :, p0:p0 + 16],
                                         fix.unsqueeze(1).to_broadcast([P, 2, 16]), ALU.mult))
                own()
                V.scalar_tensor_tensor(two(pooled)[:, :, 0:SEQ], src[:, :, p0:p0 + SEQ], 1.0 / w,
                                       ext[:, :, POOL_BUF:POOL_BUF + SEQ], ALU.mult, ALU.subtract)
                V.scalar_tensor_tensor(two(pooled)[:, :, SEQ:T], src[:, :, d0:d0 + DEC_SEQ], 1.0 / w,
                                       ext[:, :, s0:EXT], ALU.mult, ALU.subtract).then_inc(pooled_ready, 1)

            def pool_lower(j):
                dve.wait_ge(pool_hi, j + 1)
                for m in range(2):
                    t = HEADS + 2 * j + m
                    V.scalar_tensor_tensor(tile(b_lo, t), ab[:, 2 + m, 0:T], col("pool_scale", 0, 2 * (POOL_GROUPS - 1 - j) + m),
                                           tile(b_hi, t).bitcast(F32), ALU.mult, ALU.subtract).then_inc(b_ready, 1)

            dve.wait_ge(cols_loaded, 16)
            for s in range(AHEAD):
                dve.wait_ge(x_loaded[s], 16)
                if s == 0:
                    split(Unit(s))
                for p in range(2):
                    a_lower(2 * s + p, "mix0", 2 * s + p + 1)
                if s:
                    split(Unit(s))
            dve.wait_ge(x_loaded[3], 16)
            a_lower(6, "mix0", 7)
            a_lower(7, "mix0", 8)
            V.memset(two(pool_ext, EXT)[:, :, 0:POOL_BUF], 0.0)
            dve.wait_ge(con_loaded, 16)
            for j in range(8):
                split(Unit(AHEAD + j))
                if j == 0:
                    other = work[:, heads_only:heads_only + 2 * T]
                    for p in range(4, 8):
                        dst = sq_pair if p == 4 else other
                        step.inc(V.tensor_tensor(dst, tiles(x, 2 * p), tiles(x, 2 * p), ALU.mult))
                        own()
                        if p > 4:
                            step.inc(V.tensor_tensor(sq_pair, sq_pair, other, ALU.add))
                            own()
                    V.tensor_tensor(sq_half, sq_pair[:, 0:T], sq_pair[:, T:2 * T], ALU.add).then_inc(dve_squares, 1)
                if j == 3:
                    norm(0)
                    V.tensor_tensor(cos_r, con[:, CON["cos"]:CON["cos"] + T], rt[:], ALU.mult)
                    step.inc(V.tensor_tensor(sin_r, con[:, CON["sin"]:CON["sin"] + T], rt[:], ALU.mult))
                if j == 4:
                    own()
                    ret_qk(0, 4)
                if j == 7:
                    ret_weigh(0)
            for j in range(8):
                split(Unit(8 + AHEAD + j))
                ret_tail(0, j, stored=False)
                if j == 4:
                    ret_qk(1, 12)
                if j == 7:
                    ret_weigh(1)
            with counted(dve, HEADS - 2, [(step, 2)]) as i:
                for j in range(8):
                    split(Unit(16 + AHEAD + j, i, 8))
                    ret_tail(i + 1, j)
                    if j == 4:
                        ret_qk(i + 2, i * 8 + 20)
                    if j == 7:
                        ret_weigh(i + 2)
            for j in range(16):
                split(Unit(U_POOL + AHEAD + j))
                ret_tail(HEADS - 1, j)
                if j in (4, 8, 12):
                    pool_steps(j // 4 - 1, U_POOL + j)
                if j in (9, 13, 15):
                    pool_lower((9, 13, 15).index(j))

            def out_pairs(unit0, pair0, weight, a_base, before, extra):
                for kg in range(4):
                    before(kg)
                    split(Unit(unit0 + AHEAD + kg))
                    extra(kg)
                with dve.Fori(0, 3) as i:
                    for p in range(2):
                        for kg in range(4):
                            split(Unit(unit0 + AHEAD + 4 + 4 * p + kg, i, 8))
                            if kg == 0:
                                add_to_x(i * 2 + p, p, i * 8 + (unit0 + 4 + 4 * p), i * 2 + (pair0 + 1 + p))
                            if kg == 2:
                                a_lower(i * 2 + p, weight, i * 2 + (a_base + 1 + p))
                for kg in range(4):
                    split(Unit(unit0 + AHEAD + 28 + kg))
                    if kg == 0:
                        add_to_x(6, 0, unit0 + 28, pair0 + 7)
                    if kg == 2:
                        a_lower(6, weight, a_base + 7)

            def extra_a(kg):
                if kg == 0:
                    pool_steps(3, U_POOL + 16)
                if kg == 2:
                    pool_lower(3)

            out_pairs(U_OUTA, PR_OUTA, "ffn0", 8, lambda kg: None, extra_a)

            def ffn_conv(layer, t, g, units, taken):
                used(units)
                ext, conv = two(g_ext, GE), two(g_conv, GW)
                s0 = 2 + SEQ + 2
                V.tensor_scalar(ext[:, :, 2 + SEQ:s0],
                                cols[:, bass.ds(t * 2 + COL[f"ffn_hist{layer}"], 4)]
                                .rearrange("p (m t) -> p m t", m=2), 1.0, None, ALU.mult)
                V.tensor_tensor(ext[:, :, 2:2 + SEQ], banks(0)[:, :, 0:SEQ], both(rt[:])[:, :, 0:SEQ], ALU.mult)
                V.tensor_tensor(ext[:, :, s0:GE], banks(0)[:, :, SEQ:T], both(rt[:])[:, :, SEQ:T], ALU.mult)\
                    .then_inc(pair_taken, 1)
                dve.wait_ge(pair_taken, taken)
                rows = ffn_rows[:, bass.ds(t * 4 + layer * FT * 4, 8)].rearrange("p (m g t) -> p m g t", m=2, g=2)
                for n in range(FFN_CONV):
                    for m in range(2):
                        w = col(f"ffn_w{layer}", t * 3, m * FFN_CONV + n)
                        if n == 0:
                            ins = V.tensor_scalar(conv[:, m, :], ext[:, m, 0:GW], w, col(f"ffn_b{layer}", t, m),
                                                  ALU.mult, ALU.add)
                        else:
                            if m == 0:
                                own()
                            ins = V.scalar_tensor_tensor(conv[:, m, :], ext[:, m, n:n + GW], w, conv[:, m, :],
                                                         ALU.mult, ALU.add)
                    if n < FFN_CONV - 1:
                        step.inc(ins)
                        src = ext[:, :, SEQ:SEQ + 2] if n == 0 else ext[:, :, GE - 2:GE]
                        V.tensor_scalar(rows[:, :, n, :], src, 1.0, None, ALU.mult)
                ins.then_inc(conv_ready, 1)

            def ffn_up(g, units, taken):
                used(units)
                V.tensor_tensor(two(up), banks(1), both(rt[:]), ALU.mult).then_inc(pair_taken, 1)
                dve.wait_ge(pair_taken, taken)
                dve.wait_ge(gelu_ready, g + 1)
                act_ = two(g_act, GW)
                V.tensor_tensor(two(up)[:, :, 0:SEQ], two(up)[:, :, 0:SEQ], act_[:, :, 0:SEQ], ALU.mult)
                V.tensor_tensor(two(up)[:, :, SEQ:T], two(up)[:, :, SEQ:T], act_[:, :, SEQ + 2:GW], ALU.mult)\
                    .then_inc(up_ready, 1)

            def ffn_lower(g, t):
                dve.wait_ge(up_hi, g + 1)
                V.tensor_tensor(tiles(b_lo, t), up, tiles(b_hi, t).bitcast(F32), ALU.subtract).then_inc(f_ready, 1)

            def ffn(layer, unit0, pair0, k_norm, g0, weight, next_weight, a_base):
                V.memset(two(g_ext, GE)[:, :, 0:2], 0.0)
                for b, (f, k, u0, p0, down_u, down_p) in enumerate(ffn_blocks(unit0, pair0)):
                    g = g0 + f // 2
                    for j in range(8):
                        split(Unit(u0 + AHEAD + j))
                        if j == 0:
                            add_to_x(KT // UM - 1, 1, u0, p0)
                        if j == 2 and b == 0:
                            a_lower(KT // UM - 1, weight, a_base)
                        if j == 3 and b == 0:
                            norm(k_norm)
                        if j == 4:
                            ffn_conv(layer, f, g, u0 + 4, p0 + 1)
                    with counted(dve, k // 2 - 1, [(step, 2)]) as i:
                        for j in range(8):
                            split(Unit(u0 + AHEAD + 8 + j, i, 8))
                            if j == 0:
                                ffn_up(i + g, i * 8 + (u0 + 8), i * 2 + (p0 + 2))
                            if j == 2:
                                ffn_lower(i + g, i * 2)
                            if j == 4:
                                ffn_conv(layer, i * 2 + (f + 2), i + (g + 1), i * 8 + (u0 + 12), i * 2 + (p0 + 3))
                    groups = k // UK
                    final = b == len(BLOCKS) - 1
                    for kg in range(groups):
                        split(Unit(down_u + AHEAD + kg))
                        if kg == 0:
                            ffn_up(g + k // 2 - 1, down_u, down_p)
                        if kg == 1:
                            ffn_lower(g + k // 2 - 1, k - 2)
                    if groups == 4:
                        with dve.Fori(0, 3) as i:
                            for p in range(2):
                                for kg in range(4):
                                    split(Unit(down_u + AHEAD + 4 + 4 * p + kg, i, 8))
                                    if kg == 0:
                                        add_to_x(i * 2 + p, p, i * 8 + (down_u + 4 + 4 * p),
                                                 i * 2 + (down_p + 1 + p))
                        for kg in range(4):
                            split(Unit(down_u + AHEAD + 28 + kg))
                            if kg == 0:
                                add_to_x(6, 0, down_u + 28, down_p + 7)
                    else:
                        for p in range(1, KT // UM):
                            for kg in range(groups):
                                split(Unit(down_u + AHEAD + groups * p + kg))
                                if kg == 0:
                                    add_to_x(p - 1, (p - 1) % 2, down_u + groups * p, down_p + p)
                                if kg == 2 and final and next_weight:
                                    a_lower(p - 1, next_weight, a_base + p)

            ffn(0, U_FFN0, PR_FFN0, 1, 0, "ffn0", "mix1", 16)

            for kg in range(4):
                split(Unit(U_GATES + AHEAD + kg))
                if kg == 0:
                    add_to_x(KT // UM - 1, 1, U_GATES, PR_GATES)
                if kg == 1:
                    a_lower(KT // UM - 1, "mix1", 24)
            H8 = slice(0, HEADS)
            C_S = 0.25 * DK ** -0.5
            ends = slice(SEQ - 1, T, DEC_SEQ)

            def gates(j):
                if j == 0:
                    V.memset(g_pair[0:64, :], 0.0)
                    used(U_GATES + 4)
                    V.tensor_tensor(g_i[H8, :], gb[H8, 0, 0:T], rt[H8, :], ALU.mult)
                    V.tensor_tensor(g_f[H8, :], gb[32:32 + HEADS, 0, 0:T], rt[32:32 + HEADS, :], ALU.mult)\
                        .then_inc(pair_taken, 1)
                    dve.wait_ge(pair_taken, PR_GATES + 1)
                    V.tensor_scalar(g_i[H8, :], g_i[H8, :], cols[H8, COL["b_i"]:COL["b_i"] + 1], None, ALU.add)
                    step.inc(V.tensor_scalar(g_f[H8, :], g_f[H8, :], cols[H8, COL["b_f"]:COL["b_f"] + 1], None,
                                             ALU.add))
                    own()
                    V.scalar_tensor_tensor(g_e[H8, :], g_f[H8, :], -1.0, g_f[H8, :], ALU.mult, ALU.max)\
                        .then_inc(gates_dve, 1)
                if j == 1:
                    dve.wait_ge(gates_act, 1)
                    V.tensor_scalar(g_b[H8, :], g_u[H8, :], 1.0, None, ALU.add).then_inc(gates_dve, 1)
                    dve.wait_ge(gates_dve, 2)
                    V.scalar_tensor_tensor(g_u[H8, :], g_b[H8, :], -1.0, g_u[H8, :], ALU.add, ALU.subtract)
                    step.inc(V.reciprocal(g_e[H8, :], g_b[H8, :]))
                    own()
                    step.inc(V.tensor_tensor(g_u[H8, :], g_u[H8, :], g_e[H8, :], ALU.mult))
                if j == 2:
                    dve.wait_ge(gates_act, 2)
                    own()
                    step.inc(V.tensor_tensor(g_l[H8, :], g_l[H8, :], g_u[H8, :], ALU.subtract))
                    own()
                    step.inc(V.scalar_tensor_tensor(g_f[H8, :], g_f[H8, :], 0.0, g_l[H8, :], ALU.min,
                                                    ALU.subtract))
                    own()
                    for at, end in ((0, SEQ), (SEQ, T)):
                        ins = V.tensor_tensor_scan(g_b[H8, at:end], g_f[H8, at:end], g_pair[H8, at:end], 0.0,
                                                   ALU.add, ALU.add)
                    step.inc(ins)
                    own()
                    step.inc(V.tensor_tensor(g_pair[H8, :], g_i[H8, :], g_b[H8, :], ALU.subtract))
                    own()
                    V.tensor_tensor_scan(g_rows[H8, 0:SEQ], g_pair[H8, 0:SEQ], g_pair[H8, 0:SEQ], 0.0,
                                         ALU.max, ALU.max)
                    step.inc(V.tensor_tensor_scan(g_rows[H8, SEQ:T], g_pair[H8, SEQ:T], g_pair[H8, SEQ:T],
                                                  cols[H8, COL["m0"]:COL["m0"] + 1], ALU.max, ALU.max))
                    own()
                    V.tensor_scalar(g_m[H8, 2:4], g_rows[H8, ends], -1.0, None, ALU.mult)
                    V.tensor_copy(g_rows[H8, 2 * T + 1:2 * T + 2], cols[H8, COL["m0"]:COL["m0"] + 1])
                    V.tensor_tensor(g_e[H8, :], g_b[H8, :], g_rows[H8, 0:T], ALU.add).then_inc(gates_dve, 1)
                    dve.wait_ge(gates_dve, 3)
                    V.tensor_copy(g_m[H8, 0:2], g_e[H8, ends])
                if j == 4:
                    dve.wait_ge(gates_turned, 1)
                    V.tensor_copy(g_tok[:, 0:128], ab[:, 3, 0:128])
                    V.tensor_copy(g_tok[0:DEC_SEQ, 128:192], ab[0:DEC_SEQ, 3, 128:192]).then_inc(gates_tok, 1)

            def ml_qk(h, units):
                used(units)
                ext, z = two(qk_ext, QE), two(qk, QW)
                s0 = 3 + SEQ + 3
                V.tensor_scalar(ext[:, :, 3 + SEQ:s0], cols[:, bass.ds(h * 6 + COL["conv_hist"], 6)]
                                .rearrange("p (m t) -> p m t", m=2), 1.0, None, ALU.mult)
                V.tensor_tensor(ext[:, :, 3:3 + SEQ], banks(1)[:, :, 0:SEQ], both(rt[:])[:, :, 0:SEQ], ALU.mult)
                V.tensor_tensor(ext[:, :, s0:QE], banks(1)[:, :, SEQ:T], both(rt[:])[:, :, SEQ:T], ALU.mult)\
                    .then_inc(pair_taken, 1)
                dve.wait_ge(pair_taken, h * 3 + (PR_ML + 1))
                rows = conv_rows[:, bass.ds(h * 12, 12)].rearrange("p (m g t) -> p m g t", m=2, g=2)
                for n in range(ML_CONV):
                    for m in range(2):
                        w = col("conv_c_w", h * 8, m * ML_CONV + n)
                        if n == 0:
                            ins = V.tensor_scalar(z[:, m, :], ext[:, m, 0:QW], w, col("conv_c_b", h * 2, m),
                                                  ALU.mult, ALU.add)
                        else:
                            if m == 0:
                                own()
                            ins = V.scalar_tensor_tensor(z[:, m, :], ext[:, m, n:n + QW], w, z[:, m, :],
                                                         ALU.mult, ALU.add)
                    if n < ML_CONV - 1:
                        step.inc(ins)
                    if n < 2:
                        src = ext[:, :, SEQ:SEQ + 3] if n == 0 else ext[:, :, QE - 3:QE]
                        V.tensor_scalar(rows[:, :, n, :], src, 1.0, None, ALU.mult)
                ins.then_inc(qk_conv, 1)

            def ml_mask(h):
                V.tensor_scalar(g_mask[H8, :], g_rows[H8, :], con[H8, bass.ds(h + CON["ident"], 1)], None, ALU.mult)\
                    .then_inc(g_masked, 1)

            def ml_silu(h):
                dve.wait_ge(qk_conv, h + 1)
                dve.wait_ge(qk_tanh_ready, h + 1)
                V.scalar_tensor_tensor(qk, qk_tanh, 1.0, qk, ALU.add, ALU.mult).then_inc(qk_silu, 1)

            def a_of(n, h, w, at=0):
                return g_tok[0:w, bass.ds(h + (n * 64 + at), 1)]

            def ml_late(h):
                dve.wait_ge(m_spread, h + 1)
                for n, (dst, src, w, t) in enumerate(((0, 0, P, SEQ), (SEQ, P, P, P), (SEQ + P, SEQ, DEC_SEQ, DEC_SEQ))):
                    last = V.scalar_tensor_tensor(late_x[0:w, dst:dst + t], ab[0:w, 0, src:src + t], a_of(n, h, w),
                                                  late[0:w, 0:t], ALU.subtract, ALU.max)
                last.then_inc(late_ready, 1)

            def ml_weigh(h):
                dve.wait_ge(ml_scores, h + 1)
                for n in range(3):
                    w = P if n < 2 else DEC_SEQ
                    V.tensor_scalar(kw_tok[0:w, n * P:(n + 1) * P], ab[0:w, 3, n * P:(n + 1) * P],
                                    a_of(n, h, w, 32), 0.5 * DK ** -0.5, ALU.mult, ALU.mult)
                V.tensor_scalar(n_b, ones, col("n0", h), None, ALU.mult)
                dve.wait_ge(dw_ready, h + 1)
                V.scalar_tensor_tensor(sm_t[:, 0:SEQ + P], ab[:, 2, 0:SEQ + P], C_S, dw[:, 0:SEQ + P], ALU.mult,
                                       ALU.mult)
                V.scalar_tensor_tensor(sm_t[0:DEC_SEQ, SEQ + P:SC], ab[0:DEC_SEQ, 2, SEQ + P:SC], C_S,
                                       dw[0:DEC_SEQ, SEQ + P:SC], ALU.mult, ALU.mult)
                dve.wait_ge(em_ready, h * 2 + 2)
                V.scalar_tensor_tensor(q_iw, qk[:, SEQ + 3:QW], 0.5, iw_b, ALU.mult, ALU.mult)\
                    .then_inc(ml_intra, 1)

            def ml_v(h, units):
                used(units)
                V.tensor_tensor(two(vm_t), banks(0), both(rt[:]), ALU.mult).then_inc(pair_taken, 1)

            def ml_v_tok(h):
                dve.wait_ge(vm_turned, h + 1)
                V.tensor_copy(vm_tok[:, 0:2 * ML_DV], ab[:, 0, 0:2 * ML_DV])
                V.tensor_copy(vm_tok[0:DEC_SEQ, 2 * ML_DV:3 * ML_DV], ab[0:DEC_SEQ, 1, 0:ML_DV])\
                    .then_inc(vm_tok_ready, 1)

            def ml_states(h, stored):
                dve.wait_ge(num_sq_ready, h + 1)
                V.tensor_tensor(num_sq[:, 0:T], num_sq[:, 0:T], num_sq[:, T:2 * T], ALU.add)
                if stored:
                    dve.wait_ge(c_stored, h * 16)
                decay = em_b[:, T:T + 1]
                V.tensor_copy(c_new[:, 0:ML_DV], ab[:, 3, 0:ML_DV])
                V.scalar_tensor_tensor(c_new[:, ML_DV:2 * ML_DV], c_in, decay, ab[:, 3, ML_DV:2 * ML_DV],
                                       ALU.mult, ALU.add)
                V.tensor_copy(c_new[:, 2 * ML_DV:2 * ML_DV + 1], ab[:, 2, T:T + 1])
                V.scalar_tensor_tensor(c_new[:, 2 * ML_DV + 1:2 * ML_DV + 2], n_b[:, 0:1], decay,
                                       ab[:, 2, T + 1:T + 2], ALU.mult, ALU.add).then_inc(ml_state, 1)

            def ml_floor(h):
                step.inc(V.tensor_tensor(floor_, floor_, em_b[:, 0:T], ALU.max))
                own()
                step.inc(V.scalar_tensor_tensor(floor_sq, floor_, EPS, floor_, ALU.mult, ALU.mult))

            def ml_tail(h, j):
                if j == 0:
                    dve.wait_ge(ml_std, h + 1)
                    step.inc(V.reciprocal(m_rs, m_std))
                    own()
                    for m in range(2):
                        last = V.scalar_tensor_tensor(h_n[:, m * T:(m + 1) * T], ab[:, m, 0:T],
                                                      col("ml_norm", h * 2, m), m_rs, ALU.mult, ALU.mult)
                    step.inc(last)
                if j == 1:
                    dve.wait_ge(o_tanh_ready, h + 1)
                    own()
                    V.scalar_tensor_tensor(o_z, o_tanh, 1.0, h_n, ALU.add, ALU.mult).then_inc(ml_y, 1)
                if j == 2:
                    dve.wait_ge(ml_y_hi, h + 1)
                    V.tensor_tensor(tiles(b_lo, h * 2), o_z, tiles(b_hi, h * 2).bitcast(F32), ALU.subtract)\
                        .then_inc(ml_b_ready, 1)

            def ml_o(h, units):
                used(units)
                V.tensor_tensor(two(o_z), banks(1), both(rt[:]), ALU.mult).then_inc(pair_taken, 1)

            def ml_var_of(h):
                own()
                dve.wait_ge(ml_sq_sum, h + 1)
                step.inc(V.scalar_tensor_tensor(m_std, ab[:, 2, 0:T], 1.0 / ML_DV, floor_sq, ALU.mult, ALU.add))
                own()
                V.tensor_scalar(m_std, m_std, 2.0 ** -110, 2.0 ** 110, ALU.max, ALU.min).then_inc(ml_var, 1)

            def ml_steps(h, j, units, stored):
                if j == 2 and stored:
                    ml_mask(h)
                if j == 4:
                    ml_qk(h, units(4))
                if j == 5:
                    ml_silu(h)
                if j == 6:
                    if stored:
                        ml_late(h)
                    else:
                        dve.wait_ge(gates_act, 4)
                        ml_mask(h)
                if j == 7 and not stored:
                    dve.wait_ge(gates_tok, 1)
                    ml_late(h)
                if j == 7:
                    ml_weigh(h)
                if j == 8:
                    ml_v(h, units(8))
                if j == 9:
                    ml_v_tok(h)
                if j == 10:
                    ml_states(h, stored)
                    ml_floor(h)
                if j == 11:
                    ml_var_of(h)

            V.memset(two(qk_ext, QE)[:, :, 0:3], 0.0)
            for j in range(12):
                split(Unit(U_ML + AHEAD + j))
                if j == 1:
                    norm(2)
                gates(j - 2)
                ml_steps(0, j, lambda n: U_ML + n, False)
            with counted(dve, HEADS - 1, [(step, 8)]) as i:
                for j in range(12):
                    if j == 0:
                        ml_o(i, i * 12 + (U_ML + 12))
                    split(Unit(U_ML + AHEAD + 12 + j, i, 12))
                    ml_tail(i, j)
                    ml_steps(i + 1, j, lambda n: i * 12 + (U_ML + 12 + n), True)

            def before_c(kg):
                if kg == 0:
                    ml_o(HEADS - 1, U_OUTC)

            out_pairs(U_OUTC, PR_OUTC, "ffn1", 24, before_c, lambda kg: ml_tail(HEADS - 1, kg))
            ffn(1, U_FFN1, PR_FFN1, 3, FT // 2, "ffn1", None, 32)
            add_to_x(KT // UM - 1, 1, UNITS, PR_END)
            norm(4)
            dve.wait_ge(z_ready, KT // UM)
            for q in range(4):
                y = z[:, q * 4 * T:(q + 1) * 4 * T].rearrange("p (k t) -> p k t", k=4)
                V.tensor_tensor(y, y, rt[:].unsqueeze(1).to_broadcast([P, 4, T]), ALU.mult).then_inc(y_ready, 1)
    return nc


def shape_constants():
    pos = np.arange(T, dtype=np.float32)
    assert PAST_LEN == SEQ
    inv = (1.0 / (np.float32(10000.0) ** np.linspace(0.0, 1.0, DK // 2, dtype=np.float32))).astype(np.float32)
    ang = (pos[:, None] * inv[None, :]).astype(np.float32).astype(np.float64).T
    lg = np.log1p(-(2.0 ** (-5.0 - np.arange(HEADS, dtype=np.float64))))
    con = np.zeros((P, CON.width), np.float32)

    def put(name, value, rows=P):
        at, width = CON.at[name]
        con[0:rows, at:at + width] = np.asarray(value).reshape(rows, width)

    put("cos", np.concatenate([np.cos(ang)] * 2))
    put("sin", np.concatenate([np.sin(ang), -np.sin(ang)]))
    s, t = np.arange(P)[:, None], np.arange(SEQ)[None, :]
    put("late", np.where(t >= s, 0.0, 1e4))
    put("ident", np.eye(P))
    put("ones", np.ones((P, P)))
    kdec = np.zeros((P, 3, HEADS))
    for n in range(2):
        kdec[:, n] = np.exp((SEQ - 1 - n * P - np.arange(P))[:, None] * lg) * DK ** -0.5
    kdec[:DEC_SEQ, 2] = np.exp((DEC_SEQ - 1 - np.arange(DEC_SEQ))[:, None] * lg) * DK ** -0.5
    put("kdec", kdec)
    put("gamma_l", np.tile(np.exp(DEC_SEQ * lg), (P, 1)))
    fix = np.stack([(2 << j) / np.minimum(np.arange(16) + 1, 2 << j) for j in range(POOL_GROUPS)])
    put("pool_fix", np.tile(fix.reshape(1, -1), (P, 1)))
    put("eps", np.full(P, EPS))
    put("eps4", np.full(P, 4 * EPS))
    tables = np.zeros((HEADS, P, RET_TABLE), np.float32)
    for h in range(HEADS):
        tables[h, :, 0:SEQ] = np.where(t >= s, np.exp(lg[h] * np.maximum(t - s, 0)), 0.0) * DK ** -0.5
        tables[h, :, SEQ:] = np.exp((np.arange(DEC_SEQ) + 1.0) * lg[h])[None, :]
    return con, tables


def units_of(w):
    k, m = w.shape
    return w.reshape(k // (UK * P), UK, P, m // (UM * P), UM * P).transpose(3, 0, 2, 1, 4).reshape(-1, P, UW)


def kernel(**inputs):
    import concourse.bacc as bacc
    from concourse.bass_utils import run_bass_kernel_spmd

    a = {k: np.asarray(v) for k, v in inputs.items()}
    weights = np.zeros((UNITS, P, UW), np.float32)
    w = a["w_in_a"][0]
    parts = w[:, :4 * HEADS * DK].reshape(D_MODEL, 4, HEADS, DK).transpose(0, 2, 1, 3).reshape(D_MODEL, -1)
    weights[U_HEADS:U_POOL] = units_of(parts)
    weights[U_POOL:U_OUTA] = units_of(w[:, 4 * HEADS * DK:]).reshape(POOL_GROUPS, 4, P, UW)[::-1].reshape(-1, P, UW)
    w = a["w_out_a"][0]
    turned = w[HEADS * RET_DV:].reshape(POOL_GROUPS, -1, D_MODEL)[::-1].reshape(-1, D_MODEL)
    weights[U_OUTA:U_FFN0] = units_of(np.concatenate([w[:HEADS * RET_DV], turned]))
    w = a["w_in_c"][0]
    qk_w = w[:, :2 * HEADS * DK].reshape(D_MODEL, 2, HEADS, DK).transpose(0, 2, 1, 3).reshape(D_MODEL, HEADS, 2 * DK)
    v_w = w[:, 2048:4096].reshape(D_MODEL, HEADS, ML_DV)
    o_w = w[:, 4096:6144].reshape(D_MODEL, HEADS, ML_DV)
    weights[U_ML:U_OUTC] = units_of(np.stack([qk_w, v_w, o_w], 2).reshape(D_MODEL, -1))
    g_w = w[:, 6144:].reshape(KT // UK, UK, P, 2, HEADS).transpose(0, 2, 1, 3, 4)
    gate_units = weights[U_GATES:U_ML, :, :UK * P].reshape(4, P, UK, 4, 32)
    gate_units[:, :, :, 0:2, 0:HEADS] = g_w
    weights[U_GATES:U_ML, :, :UK * P] = gate_units.reshape(4, P, UK * P)
    weights[U_OUTC:U_FFN1] = units_of(a["w_out_c"][0])
    for layer, at in ((0, U_FFN0), (1, U_FFN1)):
        f = 0
        for k in BLOCKS:
            rows = slice(f * P, (f + k) * P)
            gate, up = (units_of(a[n][layer][:, rows]).reshape(k // 2, 4, P, UW) for n in ("w_gate", "w_up"))
            n = 4 * k
            weights[at:at + n] = np.stack([gate, up], 1).reshape(n, P, UW)
            at += n
            n = KT // UM * (k // UK)
            weights[at:at + n] = units_of(a["w_down"][layer][rows])
            at += n
            f += k
    w_pool = a["w_pool"][0].reshape(POOL_GROUPS * 2, P, 2 * P).transpose(1, 0, 2).reshape(P, -1)
    x = np.concatenate([a["x_prompt"][0], a["x_sample"][0]])
    x = x.T.reshape(KT, P, T).transpose(1, 0, 2).reshape(P, -1)

    def features(v):
        v = v.reshape(-1, v.shape[-1])
        return v.T.reshape(-1, P, v.shape[0]).transpose(1, 0, 2)

    def by_head(v):
        return v.reshape(P, 2, HEADS, -1).transpose(0, 2, 1, 3)

    cols = np.zeros((P, COL.width), np.float32)

    def put(name, v, rows=P):
        at, width = COL.at[name]
        cols[0:rows, at:at + width] = v.reshape(rows, width)

    for layer in range(2):
        put(f"mix{layer}", features(a["norm_mix"][layer]))
        put(f"ffn{layer}", features(a["norm_ffn"][layer]))
        put(f"ffn_w{layer}", features(a["ffn_conv_w"][layer]))
        put(f"ffn_b{layer}", features(a["ffn_conv_b"][layer]))
        put(f"ffn_hist{layer}", features(a["cache_ffn_conv"][layer, 0]))
    put("final", features(a["norm_final"]))
    put("pool_scale", features(a["pool_scale"][0]))
    put("conv_c_w", by_head(features(a["conv_c_w"][0])))
    put("conv_c_b", by_head(features(a["conv_c_b"][0])))
    put("ml_norm", features(a["ml_norm"][0]))
    put("conv_hist", by_head(features(a["cache_mlstm_conv"][0, 0])))
    put("pool_hist", features(a["cache_pool"][0, 0]))
    put("b_i", a["b_i"][0], HEADS)
    put("b_f", a["b_f"][0], HEADS)
    put("m0", a["state_mlstm_m"][0, 0], HEADS)
    put("n0", a["state_mlstm_n"][0, 0].T)
    con, tables = shape_constants()

    nc = bacc.Bacc("TRN2", target_bir_lowering=False, num_devices=1)
    arrays, args = {}, []
    for name, v in (("x", x), ("weights", weights), ("w_pool", w_pool), ("cols", cols), ("consts", con),
                    ("ret_tables", tables), ("ret_state", a["state_ret"][0, 0]), ("ml_state", a["state_mlstm_C"][0, 0])):
        arrays[f"in_{name}"] = np.ascontiguousarray(v)
        args.append(nc.dram_tensor(f"in_{name}", v.shape, F32, kind="ExternalInput").ap())
    for name, shape in (("y", (P, KT * T)), ("ret", (HEADS, P, 2 * RET_DV)), ("pool", (P, 16 * POOL_BUF)),
                        ("c", (HEADS, P, 2 * ML_DV + 2)), ("m", (HEADS, 2)), ("conv", (P, 16 * 6)),
                        ("ffn", (P, 2 * FT * 4))):
        args.append(nc.dram_tensor(f"out_{name}", shape, F32, kind="ExternalOutput").ap())
    trunk_kernel(nc, *args)
    got = run_bass_kernel_spmd(nc, [arrays], core_ids=[0]).results[0]

    y = got["out_y"].reshape(P, KT, T).transpose(2, 1, 0).reshape(T, D_MODEL)
    ret = got["out_ret"].reshape(HEADS, P, 2, RET_DV)
    pool = got["out_pool"].reshape(P, 8, 2, POOL_BUF)
    c = got["out_c"]
    conv = got["out_conv"].reshape(P, HEADS, 2, 2, 3)
    ffn = got["out_ffn"].reshape(P, 2, FT, 2, 2)
    out = [y[None, :SEQ], y[None, SEQ:]]
    for g in range(2):
        out += [ret[None, None, :, :, g],
                pool[:, :, g].transpose(2, 1, 0).reshape(1, 1, POOL_BUF, POOL_WIDTH),
                c[None, None, :, :, g * ML_DV:(g + 1) * ML_DV],
                c[None, None, :, :, 2 * ML_DV + g],
                got["out_m"][:, g].reshape(1, 1, HEADS),
                conv[:, :, :, g].transpose(3, 2, 1, 0).reshape(1, 1, 3, 2 * HEADS * DK),
                ffn[:, :, :, g].transpose(1, 3, 2, 0).reshape(2, 1, 2, D_FF)]
    return tuple(np.ascontiguousarray(v) for v in out)
```
